# Optimizing a Trainium2 kernel written in Bass

```python
import math
import jax
import jax.numpy as jnp
from jax import lax
import numpy as np

'''One inference step of a hybrid chunk-causal streaming encoder (DEPTH layers, post-LN DeepNorm).

Per layer (parallel head groups, Hymba-style):
  proj = x @ w_in                      -> [q | k | v | u]  (3*D_ATT + D_SSM columns)
  group A (D_ATT = 1024, 16 heads x 64): chunked band attention, each frame reads its own
          64-frame chunk and the previous 8 chunks, learned per-head bias on clipped relative distance
  group B (D_SSM = 1024, 64 channel groups x 16): S5 complex-diagonal SSM (64 states per group, ZOH,
          per-group step size), associative scan over positions, Re(C h) + D u, GELU, GLU
  mix = concat(rmsnorm(A), rmsnorm(B)) @ w_out ;  x1 = LN(alpha*x + mix)
  channel mixer: PEER product-key retrieval over 128^2 single-neuron experts ; x2 = LN(alpha*x1 + peer(x1))

Inputs: x_prompt (BATCH, SEQ, D_MODEL); x_sample (DEC_BATCH, DEC_SEQ, D_MODEL);
  cache_attn_k / cache_attn_v (DEPTH, DEC_BATCH, min(8*CHUNK, PAST_LEN), N_ATT_HEADS, HEAD_DIM): newest K/V rows
  state_ssm_re / state_ssm_im (DEPTH, DEC_BATCH, N_SSM_GROUPS, SSM_STATE): carried complex SSM state
  then all weights (leading DEPTH axis).
Output tuple:
  y_prompt (BATCH, SEQ, D_MODEL), y_sample (DEC_BATCH, DEC_SEQ, D_MODEL),
  new_k_prompt, new_v_prompt (DEPTH, BATCH, min(8*CHUNK, SEQ), N_ATT_HEADS, HEAD_DIM),
  new_ssm_re_prompt, new_ssm_im_prompt (DEPTH, BATCH, N_SSM_GROUPS, SSM_STATE),
  new_k_sample, new_v_sample (DEPTH, DEC_BATCH, DEC_SEQ, N_ATT_HEADS, HEAD_DIM),
  new_ssm_re_sample, new_ssm_im_sample (DEPTH, DEC_BATCH, N_SSM_GROUPS, SSM_STATE).
'''

D_MODEL = 2048
BATCH = 1
SEQ = 512
DEPTH = 1
DEC_BATCH = 1
DEC_SEQ = 64
PAST_LEN = 512

CHUNK = 64
LEFT_CHUNKS = 8
ATT_WINDOW = LEFT_CHUNKS * CHUNK
BAND = ATT_WINDOW + CHUNK
D_ATT = D_MODEL // 2
D_SSM = D_MODEL - D_ATT
HEAD_DIM = 64
N_ATT_HEADS = D_ATT // HEAD_DIM
REL_CLIP = 2 * CHUNK
SSM_GROUP = 16
N_SSM_GROUPS = D_SSM // SSM_GROUP
SSM_STATE = 64
PEER_HEADS = 8
PEER_TOPK = 16
N_KEYS = 128
N_EXPERTS = N_KEYS * N_KEYS
PEER_DKEY = 256
PEER_DHALF = PEER_DKEY // 2
PEER_BLOCK = 128
DN_ALPHA = (2.0 * DEPTH) ** 0.25
DN_BETA = (8.0 * DEPTH) ** -0.25
LN_EPS = 1e-5
RMS_EPS = 1e-6

kernel_name = 'hybrid_stream_encoder_chunkattn_s5_peer_step'

def _layer_norm(x, g, b):
    xf = x.astype(jnp.float32)
    mu = jnp.mean(xf, axis=-1, keepdims=True)
    var = jnp.mean(jnp.square(xf - mu), axis=-1, keepdims=True)
    return ((xf - mu) * lax.rsqrt(var + LN_EPS) * g + b).astype(x.dtype)

def _rms_norm(x, g):
    xf = x.astype(jnp.float32)
    return (xf * lax.rsqrt(jnp.mean(jnp.square(xf), axis=-1, keepdims=True) + RMS_EPS) * g).astype(x.dtype)

def _rel_bias(rel_bias, q_pos, k_pos):
    idx = jnp.clip(k_pos[None, :] - q_pos[:, None], -REL_CLIP, REL_CLIP) + REL_CLIP
    return rel_bias[:, idx]

def _band_attention(q, k, v, bias, valid):
    s = jnp.einsum('bqhd,bkhd->bhqk', q, k).astype(jnp.float32) * (HEAD_DIM ** -0.5) + bias.astype(jnp.float32)
    s = jnp.where(valid[None, None, None, :], s, -1e30)
    p = jax.nn.softmax(s, axis=-1).astype(v.dtype)
    return jnp.einsum('bhqk,bkhd->bqhd', p, v)

def _prompt_attention(q, k, v, rel_bias):
    B, S, H, Dh = q.shape
    n_chunks = S // CHUNK
    pad = ((0, 0), (ATT_WINDOW, 0), (0, 0), (0, 0))
    kp = jnp.pad(k, pad)
    vp = jnp.pad(v, pad)
    q_pos = jnp.arange(CHUNK)
    k_pos = jnp.arange(BAND) - ATT_WINDOW
    bias = _rel_bias(rel_bias, q_pos, k_pos)

    def one_chunk(c):
        start = c * CHUNK
        qc = lax.dynamic_slice_in_dim(q, start, CHUNK, axis=1)
        kc = lax.dynamic_slice_in_dim(kp, start, BAND, axis=1)
        vc = lax.dynamic_slice_in_dim(vp, start, BAND, axis=1)
        valid = (start + k_pos) >= 0
        return _band_attention(qc, kc, vc, bias, valid)

    out = lax.map(one_chunk, jnp.arange(n_chunks))
    return jnp.moveaxis(out, 0, 1).reshape(B, S, H, Dh)

def _sample_attention(q, k_new, v_new, k_hist, v_hist, rel_bias):
    W = k_hist.shape[1]
    Ls = q.shape[1]
    k = jnp.concatenate([k_hist.astype(k_new.dtype), k_new], axis=1)
    v = jnp.concatenate([v_hist.astype(v_new.dtype), v_new], axis=1)
    q_pos = jnp.arange(Ls)
    k_pos = jnp.arange(W + Ls) - W
    bias = _rel_bias(rel_bias, q_pos, k_pos)
    valid = jnp.ones((W + Ls,), dtype=bool)
    return _band_attention(q, k, v, bias, valid)

def _s5(u, h0, a_re, a_im, log_dt, b_re, b_im, c_re, c_im, d, glu_w, glu_b):
    f32 = jnp.float32
    lam = lax.complex(a_re.astype(f32), a_im.astype(f32))
    dt = jnp.exp(log_dt.astype(f32))[:, None]
    a_bar = jnp.exp(lam * dt)
    b = lax.complex(b_re.astype(f32), b_im.astype(f32))
    b_bar = ((a_bar - 1.0) / lam)[..., None] * b
    uf = u.astype(f32)
    bu = jnp.einsum('gph,blgh->blgp', b_bar, uf.astype(jnp.complex64))
    bu = bu.at[:, 0].add(a_bar * h0)
    a_seq = jnp.broadcast_to(a_bar, bu.shape)

    def combine(e1, e2):
        a1, b1 = e1
        a2, b2 = e2
        return a1 * a2, a2 * b1 + b2

    _, h = lax.associative_scan(combine, (a_seq, bu), axis=1)
    c = lax.complex(c_re.astype(f32), c_im.astype(f32))
    y = jnp.einsum('ghp,blgp->blgh', c, h).real + d.astype(f32) * uf
    y = jax.nn.gelu(y, approximate=False)
    gate = jax.nn.sigmoid(jnp.einsum('blgh,ghk->blgk', y, glu_w.astype(f32)) + glu_b.astype(f32))
    return y * gate, h[:, -1]

def _peer(x, wq, keys, u_tab, v_tab):
    T, D = x.shape
    q = jnp.einsum('td,de->te', x, wq).reshape(T, PEER_HEADS, 2, PEER_DHALF)
    s = jnp.einsum('thcd,hcnd->thcn', q, keys).astype(jnp.float32)
    v1, i1 = lax.top_k(s[:, :, 0], PEER_TOPK)
    v2, i2 = lax.top_k(s[:, :, 1], PEER_TOPK)
    cand = (v1[..., :, None] + v2[..., None, :]).reshape(T, PEER_HEADS, PEER_TOPK * PEER_TOPK)
    cidx = (i1[..., :, None] * N_KEYS + i2[..., None, :]).reshape(T, PEER_HEADS, PEER_TOPK * PEER_TOPK)
    top_s, pos = lax.top_k(cand, PEER_TOPK)
    idx = jnp.take_along_axis(cidx, pos, axis=-1).reshape(T, PEER_HEADS * PEER_TOPK)
    g = jax.nn.softmax(top_s, axis=-1).reshape(T, PEER_HEADS * PEER_TOPK)
    n_blocks = -(-T // PEER_BLOCK)
    pad = n_blocks * PEER_BLOCK - T
    xb = jnp.pad(x, ((0, pad), (0, 0))).reshape(n_blocks, PEER_BLOCK, D)
    ib = jnp.pad(idx, ((0, pad), (0, 0))).reshape(n_blocks, PEER_BLOCK, PEER_HEADS * PEER_TOPK)
    gb = jnp.pad(g, ((0, pad), (0, 0))).reshape(n_blocks, PEER_BLOCK, PEER_HEADS * PEER_TOPK)

    def block(args):
        xt, it, gt = args
        a = jnp.einsum('td,tkd->tk', xt, u_tab[it])
        hid = (jax.nn.gelu(a.astype(jnp.float32), approximate=False) * gt).astype(xt.dtype)
        return jnp.einsum('tk,tkd->td', hid, v_tab[it])

    y = lax.map(block, (xb, ib, gb)).reshape(n_blocks * PEER_BLOCK, D)
    return y[:T]

def _encoder_layer(x, k_hist, v_hist, h0, w_in, rel_bias, norm_attn_g, ssm_a_re, ssm_a_im, ssm_log_dt,
                   ssm_b_re, ssm_b_im, ssm_c_re, ssm_c_im, ssm_d, ssm_glu_w, ssm_glu_b, norm_ssm_g, w_out,
                   ln1_g, ln1_b, peer_wq, peer_keys, peer_u, peer_v, ln2_g, ln2_b):
    B, L, _ = x.shape
    proj = jnp.einsum('bld,de->ble', x, w_in)
    q, k, v, u = jnp.split(proj, [D_ATT, 2 * D_ATT, 3 * D_ATT], axis=-1)
    q = q.reshape(B, L, N_ATT_HEADS, HEAD_DIM)
    k = k.reshape(B, L, N_ATT_HEADS, HEAD_DIM)
    v = v.reshape(B, L, N_ATT_HEADS, HEAD_DIM)
    if k_hist is None:
        att = _prompt_attention(q, k, v, rel_bias)
    else:
        att = _sample_attention(q, k, v, k_hist, v_hist, rel_bias)
    att = _rms_norm(att.reshape(B, L, D_ATT), norm_attn_g)
    ssm, h_last = _s5(u.reshape(B, L, N_SSM_GROUPS, SSM_GROUP), h0, ssm_a_re, ssm_a_im, ssm_log_dt,
                      ssm_b_re, ssm_b_im, ssm_c_re, ssm_c_im, ssm_d, ssm_glu_w, ssm_glu_b)
    ssm = _rms_norm(ssm.reshape(B, L, D_SSM).astype(x.dtype), norm_ssm_g)
    mix = jnp.einsum('ble,ed->bld', jnp.concatenate([att, ssm], axis=-1), w_out)
    x1 = _layer_norm(DN_ALPHA * x + mix, ln1_g, ln1_b)
    ffn = _peer(x1.reshape(B * L, D_MODEL), peer_wq, peer_keys, peer_u, peer_v).reshape(B, L, D_MODEL)
    x2 = _layer_norm(DN_ALPHA * x1 + ffn, ln2_g, ln2_b)
    return x2, k, v, h_last

def setup_inputs(seed: int = 0) -> dict:
    key = jax.random.key(seed)
    ks = jax.random.split(key, 32)
    f32 = jnp.float32
    Ld = DEPTH
    w_att = min(ATT_WINDOW, PAST_LEN)

    def nrm(k, shape, scale):
        return jax.random.normal(k, shape, f32) * scale

    inputs = {}
    inputs['x_prompt'] = nrm(ks[0], (BATCH, SEQ, D_MODEL), 1.0)
    inputs['x_sample'] = nrm(ks[1], (DEC_BATCH, DEC_SEQ, D_MODEL), 1.0)
    inputs['cache_attn_k'] = nrm(ks[2], (Ld, DEC_BATCH, w_att, N_ATT_HEADS, HEAD_DIM), 1.0)
    inputs['cache_attn_v'] = nrm(ks[3], (Ld, DEC_BATCH, w_att, N_ATT_HEADS, HEAD_DIM), 1.0)
    inputs['state_ssm_re'] = nrm(ks[4], (Ld, DEC_BATCH, N_SSM_GROUPS, SSM_STATE), 0.1)
    inputs['state_ssm_im'] = nrm(ks[5], (Ld, DEC_BATCH, N_SSM_GROUPS, SSM_STATE), 0.1)
    inputs['w_in'] = nrm(ks[6], (Ld, D_MODEL, 3 * D_ATT + D_SSM), D_MODEL ** -0.5)
    inputs['rel_bias'] = nrm(ks[7], (Ld, N_ATT_HEADS, 2 * REL_CLIP + 1), 0.1)
    inputs['norm_attn_g'] = 1.0 + nrm(ks[8], (Ld, D_ATT), 0.01)
    inputs['ssm_a_re'] = -0.5 + nrm(ks[9], (Ld, N_SSM_GROUPS, SSM_STATE), 0.01)
    inputs['ssm_a_im'] = jnp.pi * jnp.arange(SSM_STATE, dtype=f32)[None, None, :] + nrm(ks[10], (Ld, N_SSM_GROUPS, SSM_STATE), 0.01)
    inputs['ssm_log_dt'] = jax.random.uniform(ks[11], (Ld, N_SSM_GROUPS), f32, minval=math.log(1e-3), maxval=math.log(1e-1))
    inputs['ssm_b_re'] = nrm(ks[12], (Ld, N_SSM_GROUPS, SSM_STATE, SSM_GROUP), (2.0 * SSM_GROUP) ** -0.5)
    inputs['ssm_b_im'] = nrm(ks[13], (Ld, N_SSM_GROUPS, SSM_STATE, SSM_GROUP), (2.0 * SSM_GROUP) ** -0.5)
    inputs['ssm_c_re'] = nrm(ks[14], (Ld, N_SSM_GROUPS, SSM_GROUP, SSM_STATE), SSM_STATE ** -0.5)
    inputs['ssm_c_im'] = nrm(ks[15], (Ld, N_SSM_GROUPS, SSM_GROUP, SSM_STATE), SSM_STATE ** -0.5)
    inputs['ssm_d'] = nrm(ks[16], (Ld, N_SSM_GROUPS, SSM_GROUP), 1.0)
    inputs['ssm_glu_w'] = nrm(ks[17], (Ld, N_SSM_GROUPS, SSM_GROUP, SSM_GROUP), SSM_GROUP ** -0.5)
    inputs['ssm_glu_b'] = nrm(ks[18], (Ld, N_SSM_GROUPS, SSM_GROUP), 0.01)
    inputs['norm_ssm_g'] = 1.0 + nrm(ks[19], (Ld, D_SSM), 0.01)
    inputs['w_out'] = nrm(ks[20], (Ld, D_ATT + D_SSM, D_MODEL), (D_ATT + D_SSM) ** -0.5 * DN_BETA)
    inputs['ln1_g'] = 1.0 + nrm(ks[21], (Ld, D_MODEL), 0.01)
    inputs['ln1_b'] = nrm(ks[22], (Ld, D_MODEL), 0.01)
    inputs['peer_wq'] = nrm(ks[23], (Ld, D_MODEL, PEER_HEADS * PEER_DKEY), D_MODEL ** -0.5)
    inputs['peer_keys'] = nrm(ks[24], (Ld, PEER_HEADS, 2, N_KEYS, PEER_DHALF), PEER_DHALF ** -0.5)
    inputs['peer_u'] = nrm(ks[25], (Ld, N_EXPERTS, D_MODEL), D_MODEL ** -0.5)
    inputs['peer_v'] = nrm(ks[26], (Ld, N_EXPERTS, D_MODEL), DN_BETA)
    inputs['ln2_g'] = 1.0 + nrm(ks[27], (Ld, D_MODEL), 0.01)
    inputs['ln2_b'] = nrm(ks[28], (Ld, D_MODEL), 0.01)
    return inputs

def reference(x_prompt, x_sample, cache_attn_k, cache_attn_v, state_ssm_re, state_ssm_im, w_in, rel_bias,
              norm_attn_g, ssm_a_re, ssm_a_im, ssm_log_dt, ssm_b_re, ssm_b_im, ssm_c_re, ssm_c_im, ssm_d,
              ssm_glu_w, ssm_glu_b, norm_ssm_g, w_out, ln1_g, ln1_b, peer_wq, peer_keys, peer_u, peer_v,
              ln2_g, ln2_b):
    f32 = jnp.float32
    yp = x_prompt
    ys = x_sample
    keep = min(ATT_WINDOW, x_prompt.shape[1])
    kp_rows, vp_rows, hp_re, hp_im = [], [], [], []
    ks_rows, vs_rows, hs_re, hs_im = [], [], [], []
    for l in range(DEPTH):
        layer_w = (w_in[l], rel_bias[l], norm_attn_g[l], ssm_a_re[l], ssm_a_im[l], ssm_log_dt[l],
                   ssm_b_re[l], ssm_b_im[l], ssm_c_re[l], ssm_c_im[l], ssm_d[l], ssm_glu_w[l], ssm_glu_b[l],
                   norm_ssm_g[l], w_out[l], ln1_g[l], ln1_b[l], peer_wq[l], peer_keys[l], peer_u[l], peer_v[l],
                   ln2_g[l], ln2_b[l])
        h0p = jnp.zeros((x_prompt.shape[0], N_SSM_GROUPS, SSM_STATE), jnp.complex64)
        yp, kp, vp, hp = _encoder_layer(yp, None, None, h0p, *layer_w)
        h0s = lax.complex(state_ssm_re[l].astype(f32), state_ssm_im[l].astype(f32))
        ys, kn, vn, hs = _encoder_layer(ys, cache_attn_k[l], cache_attn_v[l], h0s, *layer_w)
        kp_rows.append(kp[:, -keep:])
        vp_rows.append(vp[:, -keep:])
        hp_re.append(hp.real)
        hp_im.append(hp.imag)
        ks_rows.append(kn)
        vs_rows.append(vn)
        hs_re.append(hs.real)
        hs_im.append(hs.imag)
    return (yp, ys, jnp.stack(kp_rows), jnp.stack(vp_rows), jnp.stack(hp_re), jnp.stack(hp_im),
            jnp.stack(ks_rows), jnp.stack(vs_rows), jnp.stack(hs_re), jnp.stack(hs_im))


_drawn_inputs = setup_inputs


def setup_inputs(seed=0):
    import zlib

    import numpy as np

    out = dict(_drawn_inputs(seed))
    spreads = {}
    factors = {'norm_attn_g': 12.258,
     'ssm_a_re': 61.884,
     'ssm_glu_b': 5.884,
     'norm_ssm_g': 9.463,
     'ln2_g': 179.73,
     'ln2_b': 174.433}
    for name, (base, spread) in spreads.items():
        noise = np.random.default_rng([zlib.crc32(name.encode()), seed]).standard_normal(out[name].shape)
        drawn = base * np.exp(spread * noise) if base else spread * noise
        out[name] = jnp.asarray(drawn.astype(out[name].dtype))
    for name, factor in factors.items():
        out[name] = (out[name] * factor).astype(out[name].dtype)
    return out
```

```python
import math
from contextlib import ExitStack

import numpy as np
import concourse.bass as bass
from concourse import mybir

F32 = mybir.dt.float32
U32 = mybir.dt.uint32
ALU = mybir.AluOpType
ACT = mybir.ActivationFunctionType
AX = mybir.AxisListType

P = 128
D = 2048
KT = D // P
TP, TS = 512, 64
T = TP + TS
CH = 64
H, DH = 16, 64
NPAIR = H // 2
REL = 128
EXT = 6 * P
BW = TP + P
GRP, SG, SN = 64, 16, 64
SL = 8
CP, CS = TP // SL, TS // SL
C = CP + CS
GP = GRP // 2
NW = SL + 1
SLOTS = CP + 1 + CS + 1
PH, TOPK, NKEY = 8, 16, 128
KK = PH * TOPK
TILES = [(0, P), (P, P), (2 * P, P), (3 * P, P), (4 * P, TS)]
NT = len(TILES)
STEPS = [KK, KK, KK, KK, KK // 2]
RING = 4
ALPHA = 2.0 ** 0.25
LN_EPS, RMS_EPS = 1e-5, 1e-6
NEG = -1e30
LOWEST = -3.0e38
MAGIC = 12582912.0
C1 = 6.28125
C2 = float(np.float32(2 * math.pi - C1))
C3 = float(np.float32(2 * math.pi - C1 - C2))
PI_IN = 3.1415925


class Chain:

    def __init__(self, eng, sem):
        self.eng, self.sem, self.n = eng, sem, 0

    def __call__(self, ins):
        ins.then_inc(self.sem, 1)
        self.n += 1
        self.eng.wait_ge(self.sem, self.n)

    def zero(self):
        if self.n:
            self.eng.sem_clear(self.sem)
        self.n = 0


def build(nc, a, o):
    ctx = ExitStack()
    with ctx:
        sem = lambda name: ctx.enter_context(nc.semaphore(name))
        arena = ctx.enter_context(nc.sbuf_tensor("arena", [P, 53120], F32))
        bank = [ctx.enter_context(nc.psum_tensor(f"bank{i}", [P, 512], F32)) for i in range(4)]
        acc = ctx.enter_context(nc.psum_tensor("acc", [P, 2048], F32))

        def at(off, n, parts=P):
            return arena[0:parts, off:off + n]

        X, UV, G, Q, K, V, R = 0, 9216, 14336, 18944, 23552, 28160, 32768
        W, TB, Z = 37504, 41600, 45696

        xT = at(X, KT * T).rearrange("p (k t) -> p k t", k=KT)
        uP = at(UV, 8 * T).rearrange("p (m s c) -> p m s c", m=8, s=SL)
        qkv = at(Q, 24 * T)
        wring = [at(W + 2048 * j, 2048).rearrange("p (k c) -> p k c", k=KT) for j in range(2)]
        U8 = at(G, GRP * C).rearrange("p (g c) -> p g c", g=GRP)
        Hs = at(R, 2 * GP * SLOTS).rearrange("p (r g c) -> p r g c", r=2, g=GP)
        Br, Bi, Cr, Ci = (at(TB + 512 * i, 512).rearrange("p (g h) -> p g h", g=GP) for i in range(4))
        Wr, Wi, NWi = (at(TB + 2048 + 288 * i, 288).rearrange("p (g k) -> p g k", g=GP) for i in range(3))
        sm = [at(TB + 2912 + 32 * i, 32) for i in range(30)]
        (are, aim, ldt, h0r, h0i, dt, er, th, rn, cosv, sinv, nr, den, fr, fi, ta, tb) = sm[:17]
        ident = at(Z, P)
        ones = at(Z + 128, P)
        blk = at(Z + 256, P)
        iota = at(Z + 384, TOPK)
        dvec, glub, gA, gS = (at(Z + 400 + 8 * i, 8) for i in range(4))
        eps_ln, eps_rms, halfpi = (at(Z + 432 + i, 1) for i in range(3))
        glw = at(Z + 448, 128).rearrange("p (m k) -> p m k", m=8)
        E0 = Z + 576
        Gb = [at(E0 + 256 * j, 256).rearrange("p (r k h) -> p r k h", r=2, k=SL) for j in range(2)]
        E1 = E0 + 512
        CAz = [at(E1 + 576 * j, 576).rearrange("p (r g n) -> p r g n", r=2, g=2) for j in range(2)]
        E2 = E1 + 1152
        tD = [at(E2 + 128 * j, 128).rearrange("p (k h) -> p k h", k=SL) for j in range(2)]
        tP = [at(E2 + 256 + 144 * j, 144).rearrange("p (k h) -> p k h", k=NW) for j in range(2)]
        E3 = E2 + 544
        GTz = [at(E3 + 512 * j, 512).rearrange("p (r g n) -> p r g n", r=2, g=2) for j in range(2)]
        E4 = E3 + 1024
        KE = [at(E4 + 256 * j, 256, SG) for j in range(2)]
        E5 = E4 + 512
        scP, scQ = (at(E5 + 64 * j, 64).rearrange("p (r g) -> p r g", r=2) for j in range(2))
        last = at(E5 + 128, 128).rearrange("p (s r g) -> p s r g", s=2, r=2)
        E6 = E5 + 256
        Tt = [at(E6 + 256 * j, 256).rearrange("p (g n) -> p g n", g=2) for j in range(2)]
        CAy = [at(E6 + 512 + 512 * j, 512).rearrange("p (r g n) -> p r g n", r=2, g=2) for j in range(2)]
        assert E6 + 1536 <= 53120, E6 + 1536
        relb = at(X, 257, H)
        ext = at(X + 320, EXT, H)
        zer = at(X + 1100, 896)
        qz = [at(X + 1152 * j, 1152).rearrange("p (h t) -> p h t", h=2) for j in range(2)]
        vs = at(X + 2304, T)
        Vs = [at(X + 2880 + 640 * j, 640).rearrange("p (k n) -> p k n", k=5) for j in range(2)]
        cK = [at(X + 4160 + 512 * j, 512) for j in range(2)]
        cV = [at(X + 5184 + 512 * j, 512).rearrange("p (k n) -> p k n", k=4) for j in range(2)]
        Mb = [at(X + 6208 + 1280 * j, 1280).rearrange("p (h c) -> p h c", h=2) for j in range(2)]
        St = [at(TB + 576 * j, 576) for j in range(2)]
        PT = [at(TB + 1152 + 640 * j, 640).rearrange("p (k n) -> p k n", k=5) for j in range(2)]
        GW = at(TB + 2432, 1024).rearrange("p (m n) -> p m n", m=8)
        st = [at(TB + 3456 + 4 * j, 4) for j in range(2)]
        yT = at(R, 8 * T).rearrange("p (m t) -> p m t", m=8)
        yTs = at(R, 8 * T).rearrange("p (m s c) -> p m s c", m=8, s=SL)
        sq = [at(G + 576 * j, T) for j in range(2)]
        gt = [at(G + 1152 + 576 * j, T) for j in range(2)]
        rs = [at(G + 2304 + 576 * j, T) for j in range(2)]
        attT = at(Q, 8 * T).rearrange("p (m t) -> p m t", m=8)
        mixT = at(K, KT * T).rearrange("p (m t) -> p m t", m=KT)
        x1 = at(X, NT * D).rearrange("p (t d) -> p t d", t=NT)
        xin = at(X + 10240, D)
        xhat = at(X + 12288, D)
        lng, lnb = at(G, D), at(G + 2048, D)
        qpT = mixT
        sAll = at(X + 10240, D)
        eq = at(X + 12288, D)
        ur = [at(b + 2048 * j, D) for b in (Q, R) for j in range(2)]
        vr = [at(W + 2048 * j, D) for j in range(RING)]
        cand = at(R + 4096, 256)
        cand2 = at(R + 4352, 256)
        diag = [at(Q + 4096 + 128 * j, P) for j in range(4)]
        F0 = Z + 448
        keysT = at(F0, 2048).rearrange("p (m n) -> p m n", m=16)
        dots, wts = (at(F0 + 2048 + 640 * i, 640) for i in range(2))
        idx = at(F0 + 3328, 640).bitcast(U32)
        F1 = F0 + 3968
        sh, sh2 = at(F1, 256), at(F1 + 256, 256)
        hv = at(F1 + 512, 32)
        hi = at(F1 + 544, 32).bitcast(U32)
        cv = at(F1 + 576, 16)
        ci = at(F1 + 592, 16).bitcast(U32)
        i12 = at(F1 + 608, 256).rearrange("p (c h k) -> p c h k", c=2, h=PH)
        topv = at(F1 + 864, 128).rearrange("p (h k) -> p h k", h=PH)
        topp = at(F1 + 992, 128).bitcast(U32)
        pos2 = at(F1 + 1120, 256)
        row = [at(F1 + 1376 + 128 * i, 128) for i in range(2)]
        hs8 = at(F1 + 1632, 8)
        stage = [at(F1 + 1640 + j, 1).bitcast(U32) for j in range(2 * RING)]
        bns = at(F1 + 1648, 24).rearrange("p (a b) -> p a b", a=4)
        bna = at(F1 + 1672, 2)
        lnr = at(F1 + 1674, 2)
        ident2 = at(F1 + 1704, P)
        assert F1 + 1704 + P <= 53120

        uscr = nc.dram_tensor("u_scratch", [1024, SL, C], F32).ap()
        yscr = nc.dram_tensor("y_scratch", [1024, SL, C], F32).ap()
        kext = nc.dram_tensor("kernel_scratch", [GRP, SG, 15 * SG], F32).ap()
        tscr = nc.dram_tensor("toeplitz_scratch", [GP, P, 2, P], F32).ap()
        cscr = nc.dram_tensor("c_scratch", [GP, P, 2, 2, P], F32).ap()
        escr = nc.dram_tensor("distance_scratch", [H, EXT], F32).ap()
        mscr = nc.dram_tensor("bias_scratch", [H, P, BW], F32).ap()

        ssm_in, consts_in = sem("ssm_in"), sem("consts_in")
        x_in = sem("x_in")
        w_in = [sem(f"w_in{j}") for j in range(2)]
        slab_done = sem("slab_done")
        slab_out = sem("slab_out")
        u_stored, u_moved = sem("u_stored"), sem("u_moved")
        relb_in, ext_done, ext_stored, zero_done, zeros_stored, bias_done = (
            sem(n) for n in ("relb_in", "ext_done", "ext_stored", "zero_done", "zeros_stored", "bias_done"))
        mscr_made, h0_placed = sem("mscr_made"), sem("h0_placed")
        dtx, sq_r, trig = sem("dt_ready"), sem("angles_reduced"), sem("trig_done")
        tables = sem("ssm_tables")
        g_built, ca_built = sem("g_built"), sem("ca_built")
        ca_stored = [sem(f"ca_stored{j}") for j in range(2)]
        gtr, gt_ready, s_done = sem("g_transposed"), sem("gt_ready"), sem("s_done")
        k_done, ke_ready = sem("k_done"), sem("ke_ready")
        s_out, k_out = sem("s_out"), sem("k_out")
        ke_stored = [sem(f"ke_stored{j}") for j in range(2)]
        gtz_zero = sem("gtz_zero")
        h_ready = sem("h_ready")
        t_made = sem("t_made")
        y_in = [sem(f"y_in{j}") for j in range(2)]
        y_done, y_out = sem("y_done"), sem("y_out")
        y_stored, y_moved = sem("y_stored"), sem("y_moved")
        kv_out = sem("kv_out")
        outs = sem("outputs_stored")
        a_in = [sem(f"a_in{j}") for j in range(2)]
        pair_done = sem("pair_done")
        qz_ready, vs_ready, vt_done, vt_out = sem("qz_ready"), sem("vs_ready"), sem("vt_done"), sem("vt_out")
        sc_done, sc_used, mx_ready, ex_done, p_ready, pt_done, pt_out, o_done, o_out = (
            sem(n) for n in ("sc_done", "sc_used", "mx_ready", "ex_done", "p_ready", "pt_done", "pt_out",
                             "o_done", "o_out"))
        gw_ready, yd_ready, gelu_done, gate_done, sig_done, ssm_gated = (
            sem(n) for n in ("gw_ready", "yd_ready", "gelu_done", "gate_done", "sig_done", "ssm_gated"))
        sq_ready, sq_used, ms_done, rt_done, cat_ready = (
            sem(n) for n in ("sq_ready", "sq_used", "ms_done", "rt_done", "cat_ready"))
        ln_in, xt_in, xin_free, mt_done, res_ready, var_ready, sd_ready, nb_ready, xh_ready, x1_ready, x1t_done, x1t_out = (
            sem(n) for n in ("ln_in", "xt_in", "xin_free", "mt_done", "res_ready", "var_ready", "sd_ready",
                             "nb_ready", "xh_ready", "x1_ready", "x1t_done", "x1t_out"))
        keys_in, ln2_in = sem("keys_in"), sem("ln2_in")
        score_done, score_out, score_used = sem("score_done"), sem("score_out"), sem("score_used")
        gx, ge = sem("gate_logits"), sem("gate_exp")
        idx_ready = sem("idx_ready")
        u_got = [sem(f"u_got{j}") for j in range(RING)]
        v_got = [sem(f"v_got{j}") for j in range(RING)]
        u_used, v_used = sem("u_used"), sem("v_used")
        dots_ready, act_ready, wts_ready = sem("dots_ready"), sem("act_ready"), sem("wts_ready")
        diag_ready = sem("diag_ready")
        ffn_done, ffn_read = sem("ffn_done"), sem("ffn_read")
        var2, sd2, nb2, xh2, y_ready = sem("var2"), sem("sd2"), sem("nb2"), sem("xh2"), sem("y_ready")
        dve_chain, act_chain, pool_chain = sem("dve_chain"), sem("act_chain"), sem("pool_chain")

        NU = 10

        block = ctx.enter_context(nc.Block())

        @block.sync
        def _(sp):
            def slabs(first, count):
                with sp.Fori(0, count // 2) as i:
                    for j in range(2):
                        sp.wait_ge(slab_done, first + 2 * i + j + 1)
                        sp.dma_start(wring[j].rearrange("p k c -> p (k c)"),
                                     a["w"][bass.ds(first + 2 * i + j, 1)].rearrange("a p n -> (a p) n")
                                     ).then_inc(w_in[j], 16)

            sp.wait_ge(bias_done, 1)
            sp.dma_start(xT, a["x_t"].rearrange("(k p) t -> p k t", p=P)).then_inc(x_in, 16)
            slabs(0, 32)
            sp.wait_ge(slab_done, 34)
            sp.wait_ge(mscr_made, 16)
            with sp.Fori(0, NPAIR // 2) as i:
                for b in range(2):
                    sp.wait_ge(pair_done, 2 * i + b + 1)
                    m = 2 * i + b
                    sp.dma_start(cK[b], a["ck"][bass.ds(m, 1)].rearrange("a p n -> (a p) n")).then_inc(a_in[b], 16)
                    sp.dma_start(cV[b].rearrange("p k n -> p (k n)"),
                                 a["cv"][bass.ds(m, 1)].rearrange("a p n -> (a p) n")).then_inc(a_in[b], 16)
                    sp.dma_start(Mb[b], mscr[bass.ds(2 * m, 2)].rearrange("h p c -> p h c")).then_inc(a_in[b], 16)
            slabs(32, 16)
            sp.wait_ge(cat_ready, 2)
            sp.dma_start(lng, a["ln1_g"].partition_broadcast(P)).then_inc(ln_in, 16)
            sp.dma_start(lnb, a["ln1_b"].partition_broadcast(P)).then_inc(ln_in, 16)
            for t, (t0, n) in enumerate(TILES):
                if t:
                    sp.wait_ge(xin_free, t)
                for r0 in range(0, P, n):
                    sp.dma_start(xin[r0:r0 + n], a["x_tok"][t0:t0 + n, :]).then_inc(xt_in, 16)
            slabs(48, 16)
            sp.dma_start(keysT.rearrange("p m n -> p (m n)"), a["keys_t"]).then_inc(keys_in, 16)
            sp.dma_start(ident2, a["ident2"]).then_inc(keys_in, 16)
            sp.wait_ge(x1_ready, NT)
            sp.dma_start(lng, a["ln2_g"].partition_broadcast(P)).then_inc(ln2_in, 16)
            sp.dma_start(lnb, a["ln2_b"].partition_broadcast(P)).then_inc(ln2_in, 16)
            for t, (t0, n) in enumerate(TILES):
                sp.wait_ge(y_ready, t + 1)
                sp.dma_start(o["y"][t0:t0 + n, :], x1[0:n, t, :]).then_inc(outs, 16)
            sp.wait_ge(outs, 16 * (NT + 1))
            sp.wait_ge(kv_out, 32)

        @block.gpsimd
        def _(pool):
            link = Chain(pool, pool_chain)
            pool.sem_inc(u_used, RING)
            pool.sem_inc(v_used, RING)
            pool.wait_ge(ext_done, 1)
            pool.dma_start(escr, ext).then_inc(ext_stored, 16)
            pool.wait_ge(zero_done, 1)
            pool.dma_start(kext.rearrange("(g a) h n -> (a h) g n", a=8)[:, :, 0:7 * SG],
                           zer.rearrange("p (g n) -> p g n", g=8)).then_inc(zeros_stored, 16)
            pool.wait_ge(ext_stored, 16)
            shifted = bass.AP(tensor=escr.tensor, offset=P - 1, ap=[[EXT, H], [-1, P], [1, BW]])
            pool.dma_start(mscr, shifted).then_inc(mscr_made, 16)
            pool.wait_ge(zeros_stored, 16)
            pool.sem_inc(bias_done, 1)
            link(nc.gpsimd.memset(CAz[0].rearrange("p r g n -> p (r g n)"), 0.0))
            link(nc.gpsimd.memset(CAz[1].rearrange("p r g n -> p (r g n)"), 0.0))
            pool.wait_ge(tables, 1)

            def ca_round(i):
                for b in range(2):
                    g = 2 * i + b
                    wv = lambda t: t[:, bass.ds(g, 1), :].rearrange("p a k -> p (a k)").unsqueeze(2).to_broadcast([P, NW, SG])
                    cvv = lambda t: t[:, bass.ds(g, 1), :].to_broadcast([P, NW, SG])
                    pool.wait_ge(k_done, g + 1)
                    if not (isinstance(i, int) and i == 0):
                        pool.wait_ge(ca_stored[b], 16 * i)
                    for r, (w1, c1, w2, c2) in enumerate(((Wr, Cr, NWi, Ci), (NWi, Cr, Wr, Ci))):
                        link(nc.gpsimd.tensor_tensor(tP[0], wv(w1), cvv(c1), ALU.mult))
                        link(nc.gpsimd.tensor_tensor(tP[1], wv(w2), cvv(c2), ALU.mult))
                        for g2 in range(2):
                            s = slice(64 * g2, 64 * g2 + 64)
                            dst = CAz[b][s, r, g2, :].rearrange("p (k h) -> p k h", k=NW)
                            link(nc.gpsimd.tensor_tensor(dst, tP[0][s], tP[1][s],
                                                         ALU.add if r == 0 else ALU.subtract))
                    pool.sem_inc(ca_built, 1)
                    pool.dma_start(cscr[bass.ds(g, 1)].rearrange("a p r g n -> (a p) (r g) n"),
                                   CAz[b].rearrange("p r g n -> p (r g) n")[:, :, SG:NW * SG]
                                   ).then_inc(ca_stored[b], 16)

            ca_round(0)
            link.zero()
            with pool.Fori(1, GP // 2) as i:
                ca_round(i)
                link.zero()
            for b in range(2):
                pool.wait_ge(ca_stored[b], 16 * (GP // 2))
                pool.wait_ge(ke_stored[b], 16 * (GP // 2))
            for k in range(SL):
                for g2 in range(2):
                    pool.dma_start(tscr.rearrange("a (k h) g n -> g k h a n", k=SL)[g2, k],
                                   kext.rearrange("(a g) h n -> g h a n", g=2)[g2, :, :, k * SG:k * SG + P]
                                   ).then_inc(t_made, 16)
            for t in range(SL):
                if t == 0:
                    pool.wait_ge(y_out, GP + 2)
                pool.dma_start(yscr.rearrange("(g h) s c -> s h g c", h=SG)[t],
                               U8[t * SG:(t + 1) * SG]).then_inc(y_stored, 16)
            pool.wait_ge(slab_done, 34)
            pool.wait_ge(slab_out, 34)
            for b in range(2):
                link(nc.gpsimd.memset(qz[b].rearrange("p h t -> p (h t)"), 0.0))
            link.zero()
            with pool.Fori(0, NPAIR // 2) as i:
                for b in range(2):
                    m = 2 * i + b
                    pool.wait_ge(pair_done, m + 1)
                    for hh in range(2):
                        s = slice(64 * hh, 64 * hh + 64)
                        link(nc.gpsimd.tensor_copy(qz[b][s, hh, :], qkv[s, bass.ds(m * T, T)]))
                    pool.sem_inc(qz_ready, 1)
                    pool.wait_ge(vt_done, m + 1)
                    link(nc.gpsimd.tensor_copy(vs, qkv[:, bass.ds(16 * T + m * T, T)]))
                    pool.sem_inc(vs_ready, 1)
                link.zero()
            pool.wait_ge(y_stored, 16 * SL)
            pool.dma_start(yT, yscr.rearrange("(m p) s c -> p m (s c)", p=P)).then_inc(y_moved, 16)
            table = {0: a["peer_u"], 1: a["peer_v"]}
            for seg in range(NT + 1):
                if seg < NT:
                    pool.wait_ge(idx_ready, seg + 1)
                link.zero()
                nu, nv = (STEPS[seg] if seg < NT else 0), (STEPS[seg - 1] if seg else 0)
                turns = max(nu, nv) // 8
                with pool.Fori(0, turns) as i:
                    for j in range(8):
                        for kind, t, per in ((0, seg, nu // turns), (1, seg - 1, nv // turns)):
                            if per == 0 or j * per % 8:
                                continue
                            jj = j * per // 8
                            ring, got, used = ((ur, u_got, u_used), (vr, v_got, v_used))[kind]
                            s = stage[RING * kind + jj % RING]
                            pool.wait_ge(used, t * KK + per * i + jj + 1)
                            link(nc.gpsimd.tensor_copy(s, idx[:, bass.ds(t * KK + per * i + jj, 1)]))
                            pool.indirect_dma_start(
                                out=ring[jj % RING], out_offset=None, in_=table[kind],
                                in_offset=bass.IndirectOffsetOnAxis(ap=s, axis=0)).then_inc(got[jj % RING], 16)
                    link.zero()

        @block.scalar
        def _(act):
            link = Chain(act, act_chain)
            act.sem_inc(slab_out, 2)
            act.sem_inc(pt_out, 2)
            act.sem_inc(gt_ready, 1)
            act.sem_inc(k_out, 1)
            act.sem_inc(s_out, 1)
            act.sem_inc(y_out, 2)
            act.sem_inc(vt_out, 1)
            act.sem_inc(o_out, 1)
            for name, dst in (("a_re", are), ("a_im", aim), ("log_dt", ldt), ("h0_re", h0r), ("h0_im", h0i)):
                act.dma_start(dst, a[name]).then_inc(ssm_in, 16)
            for name, dst in (("b_re", Br), ("b_im", Bi), ("c_re", Cr), ("c_im", Ci)):
                act.dma_start(dst, a[name].rearrange("p (g h) -> p g h", g=GP)).then_inc(ssm_in, 16)
            act.dma_start(relb, a["rel_bias"]).then_inc(relb_in, 16)
            for name, dst in (("ident", ident), ("block", blk), ("iota", iota), ("ssm_d", dvec), ("glu_b", glub),
                              ("g_attn", gA), ("g_ssm", gS)):
                act.dma_start(dst, a[name]).then_inc(consts_in, 16)
            act.dma_start(glw, a["glu_w"].rearrange("p (m k) -> p m k", m=8)).then_inc(consts_in, 16)
            act.wait_ge(ssm_in, 16 * 9)
            nc.scalar.activation(dt, ldt, ACT.Exp).then_inc(dtx, 1)
            act.wait_ge(sq_r, 1)
            nc.scalar.activation(er, ta, ACT.Exp).then_inc(trig, 1)
            act.wait_ge(sq_r, 2)
            nc.scalar.activation(sinv, rn, ACT.Sin).then_inc(trig, 1)
            nc.scalar.activation(cosv, tb, ACT.Sin).then_inc(trig, 1)

            def product(n, b, dst, perm, scale=1.0):
                act.wait_ge(slab_done, n + 3)
                if perm:
                    nc.scalar.copy(dst[:, :, 0:CP], bank[b][:, :].rearrange("p (c s) -> p s c", s=SL))
                    nc.scalar.copy(dst[:, :, CP:C], bank[2 + b][:, 0:TS].rearrange(
                        "p (c s) -> p s c", s=SL)).then_inc(slab_out, 1)
                else:
                    nc.scalar.activation(dst(0, TP), bank[b][:, :], ACT.Copy, scale=scale)
                    nc.scalar.activation(dst(TP, TS), bank[2 + b][:, 0:TS], ACT.Copy, scale=scale
                                         ).then_inc(slab_out, 1)

            with act.Fori(0, 4) as i:
                for b in range(2):
                    product(2 * i + b, b, uP[:, bass.ds(2 * i + b, 1)].rearrange("p m s c -> p (m s) c"), True)
            act.wait_ge(slab_out, 10)
            act.dma_start(uscr.rearrange("(m p) s c -> p m (s c)", p=P),
                          uP.rearrange("p m s c -> p m (s c)")).then_inc(u_stored, 16)
            act.wait_ge(u_stored, 16)
            for k in range(SL):
                act.dma_start(U8[k * SG:(k + 1) * SG],
                              uscr.rearrange("(g h) s c -> s h g c", h=SG)[SL - 1 - k]).then_inc(u_moved, 16)
            act.wait_ge(gtz_zero, 1)
            act.wait_ge(h0_placed, 1)

            def build_round(i):
                for b in range(2):
                    g = 2 * i + b
                    act.wait_ge(gtr, g + 1)
                    act.wait_ge(s_done, g + 1)
                    for g2 in range(2):
                        ins = nc.scalar.copy(GTz[b][:, :, g2, 64 * g2:64 * g2 + 64],
                                             bank[3][:, 0:256].rearrange("p (r n) -> p r n", r=2)[:, :, 64 * g2:64 * g2 + 64])
                    ins.then_inc(gt_ready, 1)
                    act.wait_ge(k_done, g + 3)
                    if not (isinstance(i, int) and i == 0):
                        act.wait_ge(ke_stored[b], 16 * i)
                    nc.scalar.copy(KE[b], acc[0:SG, 0:256]).then_inc(k_out, 1)
                    act.wait_ge(s_done, g + 3)
                    hview = Hs[:, :, bass.ds(g, 1), :].rearrange("p r g c -> p (r g) c")
                    sview = acc[:, 512:512 + 2 * C].rearrange("p (r c) -> p r c", r=2)
                    nc.scalar.copy(hview[:, :, 1:CP + 1], sview[:, :, 0:CP])
                    nc.scalar.copy(hview[:, :, CP + 2:SLOTS], sview[:, :, CP:C]).then_inc(s_out, 1)
                    act.wait_ge(k_out, g + 2)
                    act.dma_start(kext[bass.ds(2 * g, 2)].rearrange("g h n -> h g n")[:, :, 7 * SG:15 * SG],
                                  KE[b].rearrange("p (g n) -> p g n", g=2)).then_inc(ke_stored[b], 16)

            build_round(0)
            with act.Fori(1, GP // 2) as i:
                build_round(i)
            for lo, hi_, scale in ((0, 4, DH ** -0.5), (4, 12, 1.0)):
                with act.Fori(lo, hi_) as i:
                    for b in range(2):
                        n = 2 * i + b
                        product(8 + n, b, lambda o_, w_: qkv[:, bass.ds(n * T + o_, w_)], False, scale)
            act.wait_ge(slab_out, 34)
            act.dma_start(o["k_t"].rearrange("(m p) t -> p m t", p=P),
                          qkv[:, 8 * T:16 * T].rearrange("p (m t) -> p m t", m=8)).then_inc(kv_out, 16)
            act.dma_start(o["v_t"].rearrange("(m p) t -> p m t", p=P),
                          qkv[:, 16 * T:24 * T].rearrange("p (m t) -> p m t", m=8)).then_inc(kv_out, 16)
            act.wait_ge(h_ready, 1)
            act.dma_start(o["h"], last.rearrange("p s r g -> p (s r g)")).then_inc(outs, 16)
            act.wait_ge(t_made, 32 * SL)

            def y_load(b, g):
                act.dma_start(Tt[b].rearrange("p g n -> p (g n)"),
                              tscr[g].rearrange("a p g n -> (a p) (g n)")).then_inc(y_in[b], 16)
                act.dma_start(CAy[b].rearrange("p r g n -> p (r g n)"),
                              cscr[g].rearrange("a p r g n -> (a p) (r g n)")).then_inc(y_in[b], 16)

            for b in range(2):
                y_load(b, slice(b, b + 1))
            with act.Fori(0, GP // 2 - 1) as i:
                for b in range(2):
                    g = 2 * i + b
                    act.wait_ge(y_done, g + 1)
                    nc.scalar.copy(U8[:, bass.ds(2 * g, 2), :].rearrange("p g c -> p (g c)"),
                                   bank[b][:, 0:2 * C]).then_inc(y_out, 1)
                    y_load(b, bass.ds(g + 2, 1))
            for b in range(2):
                g = GP - 2 + b
                act.wait_ge(y_done, g + 1)
                nc.scalar.copy(U8[:, 2 * g:2 * g + 2, :].rearrange("p g c -> p (g c)"),
                               bank[b][:, 0:2 * C]).then_inc(y_out, 1)
            with act.Fori(0, NPAIR // 2) as i:
                for b in range(2):
                    m = 2 * i + b

                    def exp(u):
                        rows = TS if u % 5 == 4 else P
                        keys = T if u % 5 == 4 else P * (u % 5 + 1)
                        act.wait_ge(mx_ready, m * NU + u + 1)
                        nc.scalar.activation(St[u % 2][0:rows, 0:keys], St[u % 2][0:rows, 0:keys], ACT.Exp,
                                             bias=st[u % 2][0:rows, 1:2], accum_out=st[u % 2][0:rows, 2:3]
                                             ).then_inc(ex_done, 1)

                    act.wait_ge(vt_done, m + 2)
                    act.wait_ge(pair_done, m + 1)
                    nc.scalar.copy(Vs[b][:, 0:4, :].rearrange("p k n -> p (k n)"), acc[:, 1024:1536])
                    nc.scalar.copy(Vs[b][0:TS, 4, :], acc[0:TS, 512:640]).then_inc(vt_out, 1)
                    exp(0)
                    for u in range(NU):
                        if u + 1 < NU:
                            exp(u + 1)
                        act.wait_ge(pt_done, m * NU + u + 3)
                        act.wait_ge(o_done, m * NU + u + 1)
                        src = acc[:, 512 * (u % 2):512 * (u % 2) + 512]
                        if u % 5 < 4:
                            n = u % 5 + 1
                            ins = nc.scalar.copy(PT[u % 2][:, 0:n, :].rearrange("p k n -> p (k n)"), src[:, 0:n * P])
                        else:
                            nc.scalar.copy(PT[u % 2][:, 0:4, 0:TS],
                                           src[:, 0:4 * TS].rearrange("p (k n) -> p k n", k=4))
                            ins = nc.scalar.copy(PT[u % 2][0:TS, 4, 0:TS], src[0:TS, 256:256 + TS])
                        ins.then_inc(pt_out, 1)
                    act.wait_ge(o_done, m * NU + NU + 2)
                    nc.scalar.copy(qkv[:, bass.ds(m * T, TP)], acc[:, 1536:2048])
                    nc.scalar.copy(qkv[:, bass.ds(m * T + TP, TS)], bank[3][:, 0:TS]).then_inc(o_out, 1)
            act.wait_ge(consts_in, 16 * 8)
            for m in range(8):
                act.wait_ge(yd_ready, m + 1)
                nc.scalar.activation(yT[:, m, :], yT[:, m, :], ACT.Gelu).then_inc(gelu_done, 1)
            for m in range(8):
                act.wait_ge(gate_done, m + 1)
                if m >= 2:
                    act.wait_ge(ssm_gated, m - 1)
                nc.scalar.activation(gt[m % 2][:, 0:TP], bank[m % 2][:, :], ACT.Sigmoid, bias=glub[:, m:m + 1])
                nc.scalar.activation(gt[m % 2][:, TP:T], bank[2 + m % 2][:, 0:TS], ACT.Sigmoid,
                                     bias=glub[:, m:m + 1]).then_inc(sig_done, 1)
            act.wait_ge(o_out, NPAIR + 1)
            for n in range(16):
                src = attT[:, n, :] if n < 8 else yT[:, n - 8, :]
                if n >= 8:
                    act.wait_ge(ssm_gated, n - 7)
                if n >= 2:
                    act.wait_ge(sq_used, n - 1)
                nc.scalar.activation(sq[n % 2], src, ACT.Square).then_inc(sq_ready, 1)
            for n in range(2):
                act.wait_ge(ms_done, n + 1)
                nc.scalar.activation(rs[n][:, 0:TP], bank[n][:, :], ACT.Sqrt, bias=eps_rms, scale=1.0 / 1024)
                nc.scalar.activation(rs[n][:, TP:T], bank[2 + n][:, 0:TS], ACT.Sqrt, bias=eps_rms,
                                     scale=1.0 / 1024).then_inc(rt_done, 1)
            act.wait_ge(kv_out, 32)
            with act.Fori(0, 8) as i:
                for b in range(2):
                    n = 2 * i + b
                    product(32 + n, b, lambda o_, w_: at(K, KT * T)[:, bass.ds(n * T + o_, w_)], False)
            for t, (t0, n) in enumerate(TILES):
                act.wait_ge(var_ready, t + 1)
                nc.scalar.activation(lnr[:, 0:1], bna[:, 1:2], ACT.Sqrt, bias=eps_ln).then_inc(sd_ready, 1)
                act.wait_ge(nb_ready, t + 1)
                nc.scalar.activation(xhat, xhat, ACT.Identity, bias=lnr[:, 1:2], scale=lnr[:, 0:1]).then_inc(xh_ready, 1)
                for c in range(4):
                    act.wait_ge(x1t_done, 4 * t + c + 1)
                    for q in range(4):
                        f = 4 * c + q
                        dst = (attT if f < 8 else yT)[:, f % 8, t0:t0 + n]
                        ins = nc.scalar.copy(dst, bank[c % 2][:, P * q:P * q + n])
                    ins.then_inc(x1t_out, 1)
            with act.Fori(0, 8) as i:
                for b in range(2):
                    n = 2 * i + b
                    product(48 + n, b, lambda o_, w_: at(K, KT * T)[:, bass.ds(n * T + o_, w_)], False)

            def scores(t):
                for c in range(4):
                    act.wait_ge(score_done, 4 * t + c + 1)
                    if t and c == 0:
                        act.wait_ge(score_used, t)
                    ins = nc.scalar.copy(sAll[:, 512 * c:512 * c + 512], bank[c][:, :])
                ins.then_inc(score_out, 1)

            def gates(t):
                act.wait_ge(gx, t + 1)
                nc.scalar.activation(row[0], row[0], ACT.Exp).then_inc(ge, 1)

            def diags(t, k0, k1):
                src = ident if TILES[t][1] == P else ident2
                with act.Fori(k0 // 4, k1 // 4) as i:
                    for j in range(4):
                        act.wait_ge(v_used, t * KK + 4 * i + j + 1)
                        nc.scalar.activation(diag[j], src, ACT.Copy,
                                             scale=wts[:, bass.ds(t * KK + 4 * i + j, 1)]).then_inc(diag_ready, 1)

            scores(0)
            gates(0)
            for seg in range(NT + 1):
                if seg + 1 < NT:
                    scores(seg + 1)
                if seg:
                    act.wait_ge(wts_ready, seg)
                    diags(seg - 1, 0, STEPS[seg - 1] // 2)
                if seg + 1 < NT:
                    gates(seg + 1)
                if seg:
                    diags(seg - 1, STEPS[seg - 1] // 2, STEPS[seg - 1])
                if seg < NT:
                    n = STEPS[seg]
                    act.wait_ge(dots_ready, seg + 1)
                    nc.scalar.activation(row[1][:, 0:n], dots[:, seg * KK:seg * KK + n], ACT.Gelu).then_inc(act_ready, 1)
                if seg:
                    act.wait_ge(var2, seg)
                    nc.scalar.activation(lnr[:, 0:1], bna[:, 1:2], ACT.Sqrt, bias=eps_ln).then_inc(sd2, 1)
                    act.wait_ge(nb2, seg)
                    nc.scalar.activation(x1[:, seg - 1, :], x1[:, seg - 1, :], ACT.Identity, bias=lnr[:, 1:2],
                                         scale=lnr[:, 0:1]).then_inc(xh2, 1)

        @block.vector
        def _(dve):
            link = Chain(dve, dve_chain)
            tt, ts_, stt = nc.vector.tensor_tensor, nc.vector.tensor_scalar, nc.vector.scalar_tensor_tensor
            dve.sem_inc(sc_used, 2)
            nc.vector.memset(zer, 0.0).then_inc(zero_done, 1)
            for b in range(2):
                ins = nc.vector.memset(GTz[b].rearrange("p r g n -> p (r g n)"), 0.0)
            ins.then_inc(gtz_zero, 1)
            nc.vector.memset(eps_ln, LN_EPS)
            nc.vector.memset(eps_rms, RMS_EPS)
            link(nc.vector.memset(ones, 1.0))
            dve.wait_ge(relb_in, 16)
            link(nc.vector.tensor_copy(ext[:, 0:511], relb[:, 0:1].to_broadcast([H, 511])))
            nc.vector.tensor_copy(ext[:, 511:EXT], relb).then_inc(ext_done, 1)
            dve.wait_ge(dtx, 1)
            tt(ta, are, dt, ALU.mult).then_inc(sq_r, 1)
            link(tt(th, aim, dt, ALU.mult))
            link(ts_(nr, th, 1.0 / (2 * math.pi), MAGIC, ALU.mult, ALU.add))
            link(ts_(nr, nr, -MAGIC, None, ALU.add))
            for c in (C1, C2, C3):
                link(stt(th, nr, -c, th, ALU.mult, ALU.add))
            link(ts_(rn, th, PI_IN, -PI_IN, ALU.min, ALU.max))
            link(ts_(tb, rn, -1.0, None, ALU.mult))
            link(tt(tb, tb, rn, ALU.max))
            ts_(tb, tb, -1.0, math.pi / 2, ALU.mult, ALU.add).then_inc(sq_r, 1)
            dve.wait_ge(trig, 3)
            w = lambda t, k: t[:, :, k]
            link(nc.vector.memset(w(Wr, 0), 1.0))
            link(nc.vector.memset(w(Wi, 0), 0.0))
            link(tt(w(Wr, 1), er, cosv, ALU.mult))
            link(tt(w(Wi, 1), er, sinv, ALU.mult))
            link(ts_(nr, w(Wr, 1), -1.0, None, ALU.add))
            link(tt(ta, are, are, ALU.mult))
            link(tt(tb, aim, aim, ALU.mult))
            link(tt(den, ta, tb, ALU.add))
            link(nc.vector.reciprocal(den, den))
            link(tt(ta, nr, are, ALU.mult))
            link(tt(tb, w(Wi, 1), aim, ALU.mult))
            link(tt(ta, ta, tb, ALU.add))
            link(tt(fr, ta, den, ALU.mult))
            link(tt(ta, w(Wi, 1), are, ALU.mult))
            link(tt(tb, nr, aim, ALU.mult))
            link(tt(ta, ta, tb, ALU.subtract))
            link(tt(fi, ta, den, ALU.mult))
            bch = lambda t: t.unsqueeze(2).to_broadcast([P, GP, SG])
            tm = [at(Q + 512 * i, 512).rearrange("p (g h) -> p g h", g=GP) for i in range(4)]
            link(tt(tm[0], Br, bch(fr), ALU.mult))
            link(tt(tm[1], Bi, bch(fi), ALU.mult))
            link(tt(tm[2], Bi, bch(fr), ALU.mult))
            link(tt(tm[3], Br, bch(fi), ALU.mult))
            link(tt(Br, tm[0], tm[1], ALU.subtract))
            link(tt(Bi, tm[2], tm[3], ALU.add))
            for k in range(1, SL):
                link(tt(ta, w(Wr, k), w(Wr, 1), ALU.mult))
                link(tt(tb, w(Wi, k), w(Wi, 1), ALU.mult))
                link(tt(w(Wr, k + 1), ta, tb, ALU.subtract))
                link(tt(ta, w(Wr, k), w(Wi, 1), ALU.mult))
                link(tt(tb, w(Wi, k), w(Wr, 1), ALU.mult))
                link(tt(w(Wi, k + 1), ta, tb, ALU.add))
            link(ts_(NWi, Wi, -1.0, None, ALU.mult))
            link(nc.vector.memset(Hs[:, :, :, 0], 0.0))
            link(nc.vector.tensor_copy(Hs[:, 0, :, CP + 1], h0r))
            link(nc.vector.tensor_copy(Hs[:, 1, :, CP + 1], h0i))
            dve.sem_inc(h0_placed, 1)
            dve.sem_inc(tables, 1)
            link.zero()
            with dve.Fori(0, GP // 2) as i:
                for b in range(2):
                    g = 2 * i + b
                    wv = lambda t: t[:, bass.ds(g, 1), 0:SL].rearrange("p a k -> p (a k)").unsqueeze(2).to_broadcast([P, SL, SG])
                    bv = lambda t: t[:, bass.ds(g, 1), :].to_broadcast([P, SL, SG])
                    dve.wait_ge(k_done, g + 1)
                    link(tt(tD[0], wv(Wr), bv(Br), ALU.mult))
                    link(tt(tD[1], wv(Wi), bv(Bi), ALU.mult))
                    link(tt(Gb[b][:, 0], tD[0], tD[1], ALU.subtract))
                    link(tt(tD[0], wv(Wr), bv(Bi), ALU.mult))
                    link(tt(tD[1], wv(Wi), bv(Br), ALU.mult))
                    link(tt(Gb[b][:, 1], tD[0], tD[1], ALU.add))
                    dve.sem_inc(g_built, 1)
                link.zero()
            dve.wait_ge(s_out, GP + 1)
            for c0, cn in ((0, CP), (CP + 1, CS)):
                link.zero()
                with dve.Fori(0, cn) as i:
                    h = Hs[:, :, :, bass.ds(c0 + i, 1)].rearrange("p r g c -> p r (g c)")
                    nxt = Hs[:, :, :, bass.ds(c0 + 1 + i, 1)].rearrange("p r g c -> p r (g c)")
                    w8 = lambda t: t[:, :, SL].unsqueeze(1).to_broadcast([P, 2, GP])
                    link(tt(scP, h, w8(Wr), ALU.mult))
                    link(tt(scQ, h, w8(Wi), ALU.mult))
                    link(tt(scP, scP, nxt, ALU.add))
                    link(tt(nxt[:, 0], scP[:, 0], scQ[:, 1], ALU.subtract))
                    link(tt(nxt[:, 1], scP[:, 1], scQ[:, 0], ALU.add))
                    link.zero()
            link(nc.vector.tensor_copy(last[:, 0], Hs[:, :, :, CP]))
            link(nc.vector.tensor_copy(last[:, 1], Hs[:, :, :, SLOTS - 1]))
            hm = at(E0, 2 * GP * CS).rearrange("p (r g c) -> p r g c", r=2, g=GP)
            link(nc.vector.tensor_copy(hm[:, 0], Hs[:, 0, :, CP + 1:CP + 1 + CS]))
            link(nc.vector.tensor_copy(hm[:, 1], Hs[:, 1, :, CP + 1:CP + 1 + CS]))
            link(nc.vector.tensor_copy(Hs[:, 0, :, CP:C], hm[:, 0]))
            link(nc.vector.tensor_copy(Hs[:, 1, :, CP:C], hm[:, 1]))
            dve.sem_inc(h_ready, 1)
            link.zero()
            with dve.Fori(0, NPAIR // 2) as i:
                for b in range(2):
                    m = 2 * i + b
                    dve.wait_ge(a_in[b], 48 * i + 48)
                    link(nc.vector.memset(Mb[b][0:CH, :, BW - CH:BW], NEG))

                    def front(u):
                        hh, j = divmod(u, 5)
                        rows, keys = (P, P * (j + 1)) if j < 4 else (TS, T)
                        S, stat = St[u % 2][0:rows], st[u % 2][0:rows]
                        dve.wait_ge(sc_done, m * NU + u + 1)
                        dve.wait_ge(pt_done, m * NU + u + 1)
                        if j < 4:
                            link(tt(S[:, 0:keys], bank[u % 2][:, 0:keys], Mb[b][:, hh, TP - P * j:BW], ALU.add))
                        else:
                            tt(S[:, 0:TP], bank[u % 2][0:TS, :], Mb[b][0:TS, hh, 0:TP], ALU.add)
                            link(tt(S[:, TP:T], bank[2][0:TS, 0:TS], Mb[b][0:TS, hh, TP:T], ALU.add))
                        dve.sem_inc(sc_used, 1)
                        link(nc.vector.reduce_max(stat[:, 0:1], S[:, 0:keys], AX.X))
                        ts_(stat[:, 1:2], stat[:, 0:1], -1.0, None, ALU.mult).then_inc(mx_ready, 1)

                    def back(u):
                        j = u % 5
                        rows, keys = (P, P * (j + 1)) if j < 4 else (TS, T)
                        S, stat = St[u % 2][0:rows], st[u % 2][0:rows]
                        dve.wait_ge(ex_done, m * NU + u + 1)
                        link(nc.vector.reciprocal(stat[:, 3:4], stat[:, 2:3]))
                        ts_(S[:, 0:keys], S[:, 0:keys], stat[:, 3:4], None, ALU.mult).then_inc(p_ready, 1)

                    front(0)
                    for u in range(NU):
                        if u + 1 < NU:
                            front(u + 1)
                        back(u)
                link.zero()
            dve.wait_ge(consts_in, 16 * 8)
            for m in range(8):
                ins = tt(GW[:, m, :].rearrange("p (g k) -> p g k", g=8),
                         glw[:, m, :].unsqueeze(1).to_broadcast([P, 8, SG]),
                         blk.rearrange("p (g k) -> p g k", g=8), ALU.mult)
            ins.then_inc(gw_ready, 1)
            dve.wait_ge(y_moved, 16)
            for m in range(8):
                stt(yT[:, m, :], uP[:, m].rearrange("p s c -> p (s c)"), dvec[:, m:m + 1], yT[:, m, :],
                    ALU.mult, ALU.add).then_inc(yd_ready, 1)
            for m in range(8):
                dve.wait_ge(sig_done, m + 1)
                tt(yT[:, m, :], yT[:, m, :], gt[m % 2], ALU.mult).then_inc(ssm_gated, 1)
            for n in range(2):
                dve.wait_ge(rt_done, n + 1)
                link(nc.vector.reciprocal(rs[n], rs[n]))
                for m in range(8):
                    if n == 0:
                        ins = stt(attT[:, m, :], attT[:, m, :], gA[:, m:m + 1], rs[0], ALU.mult, ALU.mult)
                    else:
                        tmp = gt[m % 2]
                        link(stt(tmp, yT[:, m, :], gS[:, m:m + 1], rs[1], ALU.mult, ALU.mult))
                        v = tmp.rearrange("p (s c) -> p s c", s=SL)
                        nc.vector.tensor_copy(yT[:, m, 0:TP].rearrange("p (c s) -> p s c", s=SL), v[:, :, 0:CP])
                        ins = nc.vector.tensor_copy(yT[:, m, TP:T].rearrange("p (c s) -> p s c", s=SL), v[:, :, CP:C])
                        if m < 7:
                            link(ins)
                ins.then_inc(cat_ready, 1)

            def norm(xv, var, sd, nb, xh, ready, t):
                for c in range(4):
                    ins = nc.vector.bn_stats(bns[:, c, :], xv[:, 512 * c:512 * c + 512])
                link(ins)
                nc.vector.bn_aggr(bna, bns.rearrange("p a b -> p (a b)")).then_inc(var, 1)
                dve.wait_ge(sd, t + 1)
                link(nc.vector.reciprocal(lnr[:, 0:1], lnr[:, 0:1]))
                stt(lnr[:, 1:2], bna[:, 0:1], -1.0, lnr[:, 0:1], ALU.mult, ALU.mult).then_inc(nb, 1)
                dve.wait_ge(xh, t + 1)

            dve.wait_ge(ln_in, 32)
            for t, (t0, n) in enumerate(TILES):
                dve.wait_ge(xt_in, 16 * (t + 1 if n == P else t + 2))
                dve.wait_ge(mt_done, t + 1)
                ins = stt(xhat, xin, ALPHA, acc[:, :], ALU.mult, ALU.add)
                ins.then_inc(res_ready, 1)
                dve.wait_ge(res_ready, t + 1)
                dve.sem_inc(xin_free, 1)
                norm(xhat, var_ready, sd_ready, nb_ready, xh_ready, x1_ready, t)
                link(tt(xhat, xhat, lng, ALU.mult))
                tt(x1[:, t, :], xhat, lnb, ALU.add).then_inc(x1_ready, 1)

            def head(t, h, first):
                s, s2 = sh, sh2
                link(nc.vector.tensor_copy(s, sAll[:, bass.ds(h * 256, 256)]))
                for c in range(2):
                    v, ix = hv[:, 16 * c:16 * c + 16], hi[:, 16 * c:16 * c + 16]
                    sc_, sc2 = s[:, P * c:P * c + P], s2[:, P * c:P * c + P]
                    top16(v, ix, sc_, sc2)
                cd = cand.rearrange("p (a b) -> p a b", a=TOPK)
                link(tt(cd, hv[:, 0:16].unsqueeze(2).to_broadcast([P, TOPK, TOPK]),
                        hv[:, 16:32].unsqueeze(1).to_broadcast([P, TOPK, TOPK]), ALU.add))
                top16(cv, ci, cand, cand2)
                for c in range(2):
                    link(nc.vector.tensor_copy(i12[:, c, bass.ds(h, 1), :].rearrange("p h k -> p (h k)"),
                                               hi[:, 16 * c:16 * c + 16]))
                link(nc.vector.tensor_copy(topv[:, bass.ds(h, 1), :].rearrange("p h k -> p (h k)"), cv))
                link(nc.vector.tensor_copy(topp[:, bass.ds(h * 16, 16)], ci))

            def top16(v, ix, x, x2):
                link(nc.vector.max(v[:, 0:8], x))
                link(nc.vector.max_index(ix[:, 0:8], v[:, 0:8], x))
                link(nc.vector.match_replace(x2, v[:, 0:8], x, LOWEST))
                link(nc.vector.max(v[:, 8:16], x2))
                link(nc.vector.max_index(ix[:, 8:16], v[:, 8:16], x2))
            HEAD = 1 + 15 + 1 + 4

            def decode(t):
                dve.sem_inc(score_used, 1)
                pu = pos2.bitcast(U32)
                link(nc.vector.tensor_scalar(pu[:, 0:KK], topp, 4, None, ALU.logical_shift_right))
                link(nc.vector.tensor_scalar(pu[:, KK:2 * KK], topp, 15, None, ALU.bitwise_and))
                link(nc.vector.tensor_copy(pos2, pu))
                full = [P, PH, TOPK, TOPK]
                e4 = eq.rearrange("p (h k j) -> p h k j", h=PH, k=TOPK)
                for c in range(2):
                    pc = pos2[:, KK * c:KK * c + KK].rearrange("p (h k) -> p h k", h=PH)
                    link(tt(e4, pc.unsqueeze(3).to_broadcast(full),
                            iota.unsqueeze(1).unsqueeze(1).to_broadcast(full), ALU.is_equal))
                    link(tt(e4, e4, i12[:, c].unsqueeze(2).to_broadcast(full), ALU.mult))
                    link(nc.vector.reduce_sum(row[c], eq.rearrange("p (k j) -> p k j", j=TOPK), AX.X))
                link(stt(idx[:, t * KK:(t + 1) * KK], row[0], float(NKEY), row[1], ALU.mult, ALU.add))
                if STEPS[t] < KK:
                    link(nc.vector.tensor_copy(idx[TS:P, t * KK:t * KK + STEPS[t]],
                                               idx[TS:P, t * KK + STEPS[t]:(t + 1) * KK]))
                dve.sem_inc(idx_ready, 1)
                rv = row[0].rearrange("p (h k) -> p h k", h=PH)
                tt(rv, topv, topv[:, :, 0:1].to_broadcast([P, PH, TOPK]), ALU.subtract).then_inc(gx, 1)
                dve.wait_ge(ge, t + 1)
                link(nc.vector.reduce_sum(hs8, rv, AX.X))
                link(nc.vector.reciprocal(hs8, hs8))
                link(tt(wts[:, t * KK:(t + 1) * KK].rearrange("p (h k) -> p h k", h=PH), rv,
                        hs8.unsqueeze(2).to_broadcast([P, PH, TOPK]), ALU.mult))
                if STEPS[t] < KK:
                    link(nc.vector.tensor_copy(wts[TS:P, t * KK:t * KK + STEPS[t]],
                                               wts[TS:P, t * KK + STEPS[t]:(t + 1) * KK]))

            def dot(t, i4, j):
                dve.wait_ge(u_got[j], 16 * (t * (KK // RING) + i4 + 1))
                stt(ur[j], ur[j], 1.0, x1[:, t, :], ALU.mult, ALU.mult,
                    accum_out=dots[:, bass.ds(t * KK + RING * i4 + j, 1)]).then_inc(u_used, 1)

            dve.wait_ge(score_out, 1)
            link.zero()
            with dve.Fori(0, PH) as h:
                head(0, h, True)
                link.zero()
            decode(0)
            dve.wait_ge(ln2_in, 32)
            for seg in range(NT + 1):
                if seg < NT:
                    more = seg + 1 < NT
                    if more:
                        dve.wait_ge(score_out, seg + 2)
                    link.zero()
                    with dve.Fori(0, PH) as h:
                        if more:
                            head(seg + 1, h, False)
                        for q in range(2):
                            for j in range(RING):
                                dot(seg, 2 * h + q, j)
                        if more:
                            link.zero()
                    if more:
                        decode(seg + 1)
                    if STEPS[seg] == KK:
                        with dve.Fori(16, 32) as i:
                            for j in range(RING):
                                dot(seg, i, j)
                    n = STEPS[seg]
                    dve.wait_ge(u_used, seg * KK + n + RING)
                    dve.sem_inc(dots_ready, 1)
                    dve.wait_ge(act_ready, seg + 1)
                    wv_ = wts[:, seg * KK:seg * KK + n]
                    link(tt(wv_, wv_, row[1][:, 0:n], ALU.mult))
                    dve.sem_inc(wts_ready, 1)
                if seg:
                    t = seg - 1
                    dve.wait_ge(ffn_done, seg)
                    xv = x1[:, t, :]
                    link(stt(xv, xv, ALPHA, acc[:, :], ALU.mult, ALU.add))
                    dve.sem_inc(ffn_read, 1)
                    norm(xv, var2, sd2, nb2, xh2, y_ready, t)
                    link(tt(xv, xv, lng, ALU.mult))
                    tt(xv, xv, lnb, ALU.add).then_inc(y_ready, 1)

        @block.tensor
        def _(pe):
            mm = nc.tensor.matmul

            def carrier():
                mm(bank[2][:, 400:402], ident, ident[:, 0:2], start=True, stop=True)

            pe.sem_inc(slab_done, 2)
            pe.sem_inc(k_done, 2)
            pe.sem_inc(s_done, 2)
            pe.sem_inc(pair_done, 2)
            pe.sem_inc(vt_done, 1)
            pe.sem_inc(pt_done, 2)
            pe.sem_inc(o_done, 2)
            pe.wait_ge(x_in, 16)

            def gemm(first, count, rhs):
                with pe.Fori(0, count // 2) as i:
                    for b in range(2):
                        pe.wait_ge(w_in[b], 16 * (first // 2 + 1 + i))
                        pe.wait_ge(slab_out, first + 2 * i + b + 1)
                        for k in range(KT):
                            mm(bank[b][:, :], wring[b][:, k, :], rhs(k)[:, 0:TP], start=k == 0, stop=k == KT - 1)
                            ins = mm(bank[2 + b][:, 0:TS], wring[b][:, k, :], rhs(k)[:, TP:T],
                                     start=k == 0, stop=k == KT - 1)
                        ins.then_inc(slab_done, 1)

            gemm(0, 8, lambda k: xT[:, k, :])
            pe.wait_ge(u_moved, 16 * SL)
            pe.wait_ge(consts_in, 16 * 8)
            with pe.Fori(0, GP // 2) as i:
                for b in range(2):
                    g = 2 * i + b
                    pe.wait_ge(g_built, g + 1)
                    pe.wait_ge(gt_ready, g + 1)
                    for r in range(2):
                        ins = nc.tensor.transpose(bank[3][:, P * r:P * r + P],
                                                  Gb[b][:, r].rearrange("p k h -> p (k h)"), ident)
                    ins.then_inc(gtr, 1)
                    pe.wait_ge(ca_built, g + 1)
                    pe.wait_ge(k_out, g + 1)
                    for r in range(2):
                        ins = mm(acc[0:SG, 0:256].rearrange("p (g n) -> p g n", g=2), Gb[b][:, r, 0, :],
                                 CAz[b][:, r, :, 0:P], start=r == 0, stop=r == 1)
                    ins.then_inc(k_done, 1)
                    pe.wait_ge(gt_ready, g + 2)
                    pe.wait_ge(s_out, g + 1)
                    for r in range(2):
                        for g2 in range(2):
                            ins = mm(acc[:, 512 + C * r:512 + C * r + C], GTz[b][:, r, g2, :],
                                     U8[:, bass.ds(2 * g + g2, 1), :].rearrange("p g c -> p (g c)"),
                                     start=g2 == 0, stop=g2 == 1)
                    ins.then_inc(s_done, 1)
            gemm(8, 24, lambda k: xT[:, k, :])
            pe.wait_ge(h_ready, 1)
            with pe.Fori(0, GP // 2) as i:
                for b in range(2):
                    g = 2 * i + b
                    pe.wait_ge(y_in[b], 32 * i + 32)
                    pe.wait_ge(y_out, g + 1)
                    for g2 in range(2):
                        dst = bank[b][:, C * g2:C * g2 + C]
                        mm(dst, Tt[b][:, g2, :], U8[:, bass.ds(2 * g + g2, 1), :].rearrange("p g c -> p (g c)"),
                           start=True, stop=False)
                        for r in range(2):
                            ins = mm(dst, CAy[b][:, r, g2, :],
                                     Hs[:, r, bass.ds(g, 1), 0:C].rearrange("p g c -> p (g c)"),
                                     start=False, stop=r == 1)
                    ins.then_inc(y_done, 1)
            pe.wait_ge(y_out, GP + 2)
            with pe.Fori(0, NPAIR // 2) as i:
                for b in range(2):
                    m = 2 * i + b
                    kT = lambda n: qkv[:, bass.ds(8 * T + m * T, n)]
                    kTs = qkv[:, bass.ds(8 * T + m * T + TP, TS)]

                    def score(u):
                        hh, j = divmod(u, 5)
                        pe.wait_ge(sc_used, m * NU + u + 1)
                        if j < 4:
                            ins = mm(bank[u % 2][:, 0:P * (j + 1)], qz[b][:, hh, P * j:P * j + P], kT(P * (j + 1)),
                                     start=True, stop=True)
                        else:
                            mm(bank[u % 2][0:TS, :], qz[b][:, hh, TP:T], cK[b], start=True, stop=True)
                            ins = mm(bank[2][0:TS, 0:TS], qz[b][:, hh, TP:T], kTs, start=True, stop=True)
                        ins.then_inc(sc_done, 1)

                    pe.wait_ge(vs_ready, m + 1)
                    pe.wait_ge(vt_out, m + 1)
                    for k in range(4):
                        nc.tensor.transpose(acc[:, 1024 + P * k:1024 + P * k + P], vs[:, P * k:P * k + P], ident)
                    nc.tensor.transpose(acc[0:TS, 512:640], vs[:, TP:T], ident).then_inc(vt_done, 1)
                    pe.wait_ge(qz_ready, m + 1)
                    pe.wait_ge(a_in[b], 48 * i + 48)
                    score(0)
                    score(1)
                    for u in range(NU):
                        hh, j = divmod(u, 5)
                        S, tp = St[u % 2], acc[:, 512 * (u % 2):512 * (u % 2) + 512]
                        pe.wait_ge(p_ready, m * NU + u + 1)
                        pe.wait_ge(pt_out, m * NU + u + 1)
                        if j < 4:
                            for k in range(j + 1):
                                ins = nc.tensor.transpose(tp[:, P * k:P * k + P], S[:, P * k:P * k + P], ident)
                        else:
                            carrier()
                            for k in range(4):
                                nc.tensor.transpose(tp[:, TS * k:TS * k + TS], S[0:TS, P * k:P * k + P],
                                                    ident[0:TS, 0:TS])
                            ins = nc.tensor.transpose(tp[0:TS, 256:256 + TS], S[0:TS, TP:T], ident[0:TS, 0:TS])
                        ins.then_inc(pt_done, 1)
                        if u + 2 < NU:
                            score(u + 2)
                        if u == 0:
                            pe.wait_ge(vt_out, m + 2)
                            pe.wait_ge(o_out, m + 1)
                        pe.wait_ge(pt_out, m * NU + u + 3)
                        hs_ = slice(64 * hh, 64 * hh + 64)
                        if j < 4:
                            for k in range(j + 1):
                                ins = mm(acc[hs_, 1536 + P * j:1536 + P * j + P], Vs[b][:, k, hs_], PT[u % 2][:, k, :],
                                         start=k == 0, stop=k == j)
                        else:
                            for k in range(4):
                                mm(bank[3][hs_, 0:TS], cV[b][:, k, hs_], PT[u % 2][:, k, 0:TS], start=k == 0, stop=False)
                            ins = mm(bank[3][hs_, 0:TS], Vs[b][0:TS, 4, hs_], PT[u % 2][0:TS, 4, 0:TS],
                                     start=False, stop=True)
                        ins.then_inc(o_done, 1)
                    pe.wait_ge(o_done, m * NU + NU + 2)
                    pe.sem_inc(pair_done, 1)
            pe.wait_ge(gw_ready, 1)
            for m in range(8):
                pe.wait_ge(gelu_done, m + 1)
                if m >= 2:
                    pe.wait_ge(sig_done, m - 1)
                mm(bank[m % 2][:, :], GW[:, m, :], yT[:, m, 0:TP], start=True, stop=True)
                mm(bank[2 + m % 2][:, 0:TS], GW[:, m, :], yT[:, m, TP:T],
                   start=True, stop=True).then_inc(gate_done, 1)
            pe.wait_ge(sig_done, 8)
            for n in range(16):
                b = n // 8
                pe.wait_ge(sq_ready, n + 1)
                mm(bank[b][:, :], ones, sq[n % 2][:, 0:TP], start=n % 8 == 0, stop=n % 8 == 7)
                ins = mm(bank[2 + b][:, 0:TS], ones, sq[n % 2][:, TP:T], start=n % 8 == 0, stop=n % 8 == 7)
                ins.then_inc(sq_used, 1)
                if n % 8 == 7:
                    pe.wait_ge(sq_used, n + 1)
                    pe.sem_inc(ms_done, 1)
            pe.wait_ge(cat_ready, 2)
            cat = lambda k: (attT if k < 8 else yT)[:, k % 8, :]
            gemm(32, 16, cat)
            pe.wait_ge(slab_out, 50)
            for t, (t0, n) in enumerate(TILES):
                if t:
                    pe.wait_ge(res_ready, t)
                for f in range(KT):
                    ins = nc.tensor.transpose(acc[0:n, P * f:P * f + P], mixT[:, f, t0:t0 + n], ident)
                    if n < P:
                        ins = mm(acc[n:P, P * f:P * f + P], mixT[:, f, t0:t0 + n], ident, start=True, stop=True)
                ins.then_inc(mt_done, 1)
                pe.wait_ge(x1_ready, t + 1)
                for c in range(4):
                    if 4 * t + c >= 2:
                        pe.wait_ge(x1t_out, 4 * t + c - 1)
                    for q in range(4):
                        f = 4 * c + q
                        ins = nc.tensor.transpose(bank[c % 2][:, P * q:P * q + P], x1[:, t, P * f:P * f + P], ident)
                    ins.then_inc(x1t_done, 1)
            pe.wait_ge(x1t_out, 4 * NT)
            gemm(48, 16, cat)
            pe.wait_ge(slab_out, 66)
            pe.wait_ge(keys_in, 32)

            def scores(t):
                t0, n = TILES[t]
                if t:
                    pe.wait_ge(score_out, t)
                for c in range(4):
                    for q in range(4):
                        for r0 in range(0, P, n):
                            ins = mm(bank[c][r0:r0 + n, P * q:P * q + P], qpT[:, 4 * c + q, t0:t0 + n],
                                     keysT[:, 4 * c + q, :], start=True, stop=True)
                    ins.then_inc(score_done, 1)

            scores(0)
            for seg in range(NT + 1):
                if seg + 1 < NT:
                    scores(seg + 1)
                if seg:
                    t = seg - 1
                    turns = STEPS[t] // RING
                    if t:
                        pe.wait_ge(ffn_read, t)

                    def step(i, j, first, final):
                        k = t * KK + RING * i + j
                        pe.wait_ge(diag_ready, k + 1)
                        pe.wait_ge(v_got[j], 16 * (t * (KK // RING) + i + 1))
                        for c in range(4):
                            ins = mm(acc[:, 512 * c:512 * c + 512], diag[j], vr[j][:, 512 * c:512 * c + 512],
                                     start=first, stop=final)
                        ins.then_inc(v_used, 1)

                    for j in range(RING):
                        step(0, j, j == 0, False)
                    with pe.Fori(1, turns - 1) as i:
                        for j in range(RING):
                            step(i, j, False, False)
                    for j in range(RING):
                        step(turns - 1, j, False, j == RING - 1)
                    pe.wait_ge(v_used, t * KK + STEPS[t] + RING)
                    pe.sem_inc(ffn_done, 1)


_INS = ["x_t", "x_tok", "w", "a_re", "a_im", "log_dt", "h0_re", "h0_im", "b_re", "b_im", "c_re", "c_im",
        "rel_bias", "ident", "block", "iota", "ssm_d", "glu_b", "g_attn", "g_ssm", "glu_w", "ck", "cv",
        "ln1_g", "ln1_b", "ln2_g", "ln2_b", "ident2", "keys_t", "peer_u", "peer_v"]
_OUTS = {"y": (T, D), "k_t": (1024, T), "v_t": (1024, T), "h": (P, 128)}


def _layouts(i):
    f = {k: np.asarray(v) for k, v in i.items()}
    tok = np.concatenate([f["x_prompt"][0], f["x_sample"][0]], axis=0)
    slab = lambda w: w.reshape(KT, P, -1, P).transpose(2, 1, 0, 3).reshape(-1, P, D)
    w_in = slab(f["w_in"][0])
    pair = lambda x: x.reshape(GP, 2 * SN).T
    pairh = lambda x: x.reshape(GP, 2 * SN, SG).transpose(1, 0, 2).reshape(P, GP * SG)
    feat = lambda x: x.reshape(8, P).T
    return {
        "x_t": tok.T, "x_tok": tok,
        "w": np.concatenate([w_in[24:], w_in[:24], slab(f["w_out"][0]), slab(f["peer_wq"][0])], axis=0),
        "a_re": pair(f["ssm_a_re"][0]), "a_im": pair(f["ssm_a_im"][0]),
        "log_dt": pair(np.broadcast_to(f["ssm_log_dt"][0][:, None], (GRP, SN))),
        "h0_re": pair(f["state_ssm_re"][0, 0]), "h0_im": pair(f["state_ssm_im"][0, 0]),
        "b_re": pairh(f["ssm_b_re"][0]), "b_im": pairh(f["ssm_b_im"][0]),
        "c_re": pairh(f["ssm_c_re"][0].transpose(0, 2, 1)), "c_im": pairh(f["ssm_c_im"][0].transpose(0, 2, 1)),
        "rel_bias": f["rel_bias"][0],
        "ident": np.eye(P, dtype=np.float32), "ident2": np.tile(np.eye(TS, dtype=np.float32), (2, 2)),
        "block": np.kron(np.eye(8, dtype=np.float32), np.ones((SG, SG), np.float32)),
        "iota": np.broadcast_to(np.arange(TOPK, dtype=np.float32), (P, TOPK)),
        "ssm_d": feat(f["ssm_d"][0]), "glu_b": feat(f["ssm_glu_b"][0]),
        "g_attn": feat(f["norm_attn_g"][0]), "g_ssm": feat(f["norm_ssm_g"][0]),
        "glu_w": f["ssm_glu_w"][0].reshape(8, P, SG).transpose(1, 0, 2).reshape(P, 8 * SG),
        "ck": f["cache_attn_k"][0, 0].reshape(TP, NPAIR, P).transpose(1, 2, 0),
        "cv": f["cache_attn_v"][0, 0].reshape(4, P, NPAIR, P).transpose(2, 1, 0, 3).reshape(NPAIR, P, TP),
        "ln1_g": f["ln1_g"][0], "ln1_b": f["ln1_b"][0], "ln2_g": f["ln2_g"][0], "ln2_b": f["ln2_b"][0],
        "keys_t": f["peer_keys"][0].transpose(3, 0, 1, 2).reshape(P, 16 * NKEY),
        "peer_u": f["peer_u"][0], "peer_v": f["peer_v"][0],
    }


def kernel(**inputs):
    import concourse.bacc as bacc
    from concourse.bass_utils import run_bass_kernel_spmd

    nc = bacc.Bacc("TRN2", target_bir_lowering=False, num_devices=1)
    laid = _layouts(inputs)
    arrays, a, o = {}, {}, {}
    for name in _INS:
        x = np.ascontiguousarray(laid[name])
        arrays[f"in_{name}"] = x
        a[name] = nc.dram_tensor(f"in_{name}", x.shape, mybir.dt.from_np(x.dtype), kind="ExternalInput").ap()
    for name, shape in _OUTS.items():
        o[name] = nc.dram_tensor(f"out_{name}", shape, F32, kind="ExternalOutput").ap()
    build(nc, a, o)
    got = run_bass_kernel_spmd(nc, [arrays], core_ids=[0]).results[0]
    y, kt, vt = (np.asarray(got[f"out_{n}"]) for n in ("y", "k_t", "v_t"))
    h = np.asarray(got["out_h"]).reshape(P, 2, 2, GP).transpose(1, 2, 3, 0).reshape(2, 2, GRP, SN)
    kv = lambda x, s: np.ascontiguousarray(x[:, s].T.reshape(1, 1, -1, H, DH))
    pr, sa = slice(0, TP), slice(TP, T)
    st_ = lambda s, r: np.ascontiguousarray(h[s, r].reshape(1, 1, GRP, SN))
    return (y[None, :TP], y[None, TP:], kv(kt, pr), kv(vt, pr), st_(0, 0), st_(0, 1),
            kv(kt, sa), kv(vt, sa), st_(1, 0), st_(1, 1))
```

```python
import math
from contextlib import ExitStack

import numpy as np
import concourse.bass as bass
from concourse import mybir

F32 = mybir.dt.float32
U32 = mybir.dt.uint32
ALU = mybir.AluOpType
ACT = mybir.ActivationFunctionType
AX = mybir.AxisListType

P = 128
D = 2048
KT = D // P
TP, TS = 512, 64
T = TP + TS
CH = 64
H, DH = 16, 64
NPAIR = H // 2
REL = 128
EXT = 6 * P
BW = TP + P
GRP, SG, SN = 64, 16, 64
SL = 8
CP, CS = TP // SL, TS // SL
C = CP + CS
GP = GRP // 2
NW = SL + 1
SLOTS = CP + 1 + CS + 1
PH, TOPK, NKEY = 8, 16, 128
KK = PH * TOPK
TILES = [(0, P), (P, P), (2 * P, P), (3 * P, P), (4 * P, TS)]
NT = len(TILES)
STEPS = [KK, KK, KK, KK, KK // 2]
GROUPS = [(0, P), (P, T - P)]
FIRST = 28
DURING = 2 * (NT - 1)
LEAD = 24
RING = 4
ALPHA = 2.0 ** 0.25
LN_EPS, RMS_EPS = 1e-5, 1e-6
NEG = -1e30
LOWEST = -3.0e38
MAGIC = 12582912.0
C1 = 6.28125
C2 = float(np.float32(2 * math.pi - C1))
C3 = float(np.float32(2 * math.pi - C1 - C2))
PI_IN = 3.1415925


class Chain:

    def __init__(self, eng, sem):
        self.eng, self.sem, self.n = eng, sem, 0

    def __call__(self, ins):
        ins.then_inc(self.sem, 1)
        self.n += 1
        self.eng.wait_ge(self.sem, self.n)

    def zero(self):
        if self.n:
            self.eng.sem_clear(self.sem)
        self.n = 0


def build(nc, a, o):
    ctx = ExitStack()
    with ctx:
        sem = lambda name: ctx.enter_context(nc.semaphore(name))
        arena = ctx.enter_context(nc.sbuf_tensor("arena", [P, 53120], F32))
        bank = [ctx.enter_context(nc.psum_tensor(f"bank{i}", [P, 512], F32)) for i in range(4)]
        acc = ctx.enter_context(nc.psum_tensor("acc", [P, 2048], F32))

        gtp = [acc[:, 1024 + 512 * j:1280 + 512 * j] for j in range(2)]

        def at(off, n, parts=P):
            return arena[0:parts, off:off + n]

        X, UV, G, Q, K, V, R = 0, 9216, 14336, 18944, 23552, 28160, 32768
        W, TB, Z = 37504, 41600, 45696

        xT = at(X, KT * T).rearrange("p (k t) -> p k t", k=KT)
        uP = at(UV, 8 * T).rearrange("p (m s c) -> p m s c", m=8, s=SL)
        qkv = at(Q, 24 * T)
        wring = [at(W + 2048 * j, 2048).rearrange("p (k c) -> p k c", k=KT) for j in range(2)]
        U8 = at(G, GRP * C).rearrange("p (g c) -> p g c", g=GRP)
        Hs = at(R, 2 * GP * SLOTS).rearrange("p (r g c) -> p r g c", r=2, g=GP)
        Br, Bi, Cr, Ci = (at(TB + 512 * i, 512).rearrange("p (g h) -> p g h", g=GP) for i in range(4))
        Wr, Wi, NWi = (at(TB + 2048 + 288 * i, 288).rearrange("p (g k) -> p g k", g=GP) for i in range(3))
        sm = [at(TB + 2912 + 32 * i, 32) for i in range(30)]
        (are, aim, ldt, h0r, h0i, dt, er, th, rn, cosv, sinv, nr, den, fr, fi, ta, tb) = sm[:17]
        ident = at(Z, P)
        ones = at(Z + 128, P)
        blk = at(Z + 256, P)
        iota = at(Z + 384, TOPK)
        dvec, glub, gA, gS = (at(Z + 400 + 8 * i, 8) for i in range(4))
        eps_ln, eps_rms, halfpi = (at(Z + 432 + i, 1) for i in range(3))
        glw = at(Z + 448, 128).rearrange("p (m k) -> p m k", m=8)
        E0 = Z + 576
        Gb = [at(E0 + 256 * j, 256).rearrange("p (r k h) -> p r k h", r=2, k=SL) for j in range(2)]
        E1 = E0 + 512
        CAz = [at(E1 + 576 * j, 576).rearrange("p (r g n) -> p r g n", r=2, g=2) for j in range(2)]
        E2 = E1 + 1152
        tD = [at(E2 + 128 * j, 128).rearrange("p (k h) -> p k h", k=SL) for j in range(2)]
        tP = [at(E2 + 256 + 144 * j, 144).rearrange("p (k h) -> p k h", k=NW) for j in range(2)]
        E3 = E2 + 544
        GTz = [at(E3 + 512 * j, 512).rearrange("p (r g n) -> p r g n", r=2, g=2) for j in range(2)]
        E4 = E3 + 1024
        KE = [at(E4 + 256 * j, 256, SG) for j in range(2)]
        E5 = E4 + 512
        scP, scQ = (at(E5 + 64 * j, 64).rearrange("p (r g) -> p r g", r=2) for j in range(2))
        last = at(E5 + 128, 128).rearrange("p (s r g) -> p s r g", s=2, r=2)
        E6 = E5 + 256
        slots = (E6, E6 + 768, W, W + 768)
        Tt = [at(b, 256).rearrange("p (g n) -> p g n", g=2) for b in slots]
        CAy = [at(b + 256, 512).rearrange("p (r g n) -> p r g n", r=2, g=2) for b in slots]
        assert E6 + 1536 <= 53120, E6 + 1536
        relb = at(K, 257, H)
        ext = at(K + 320, EXT, H)
        zer = at(K + 1100, 896)
        qz = [at(X + 1152 * j, 1152).rearrange("p (h t) -> p h t", h=2) for j in range(2)]
        vs = at(X + 2304, T)
        Vs = [at(X + 2880 + 640 * j, 640).rearrange("p (k n) -> p k n", k=5) for j in range(2)]
        cK = [at(X + 4160 + 512 * j, 512) for j in range(2)]
        cV = [at(X + 5184 + 512 * j, 512).rearrange("p (k n) -> p k n", k=4) for j in range(2)]
        Mb = [at(X + 6208 + 1280 * j, 1280).rearrange("p (h c) -> p h c", h=2) for j in range(2)]
        St = [at(TB + 576 * j, 576) for j in range(2)]
        PT = [at(TB + 1152 + 640 * j, 640).rearrange("p (k n) -> p k n", k=5) for j in range(2)]
        GW = at(TB + 2432, 1024).rearrange("p (m n) -> p m n", m=8)
        st = [at(TB + 3456 + 4 * j, 4) for j in range(2)]
        yT = at(R, 8 * T).rearrange("p (m t) -> p m t", m=8)
        yTs = at(R, 8 * T).rearrange("p (m s c) -> p m s c", m=8, s=SL)
        sq = [at(G + 576 * j, T) for j in range(2)]
        gt = [at(G + 1152 + 576 * j, T) for j in range(2)]
        rs = [at(G + 2304 + 576 * j, T) for j in range(2)]
        attT = at(Q, 8 * T).rearrange("p (m t) -> p m t", m=8)
        mixT = at(K, KT * T).rearrange("p (m t) -> p m t", m=KT)
        x1 = at(X, NT * D).rearrange("p (t d) -> p t d", t=NT)
        xin = at(X + 10240, D)
        xhat = at(X + 12288, D)
        lng, lnb = at(G, D), at(G + 2048, D)
        qpT = mixT
        scored = lambda t: at(Q if t else X + 10240, D)
        onehot = lambda t: at(R if t else X + 12288, D)
        ur = [at(b, D) for b in (TB, TB + 2048, X + 10240, X + 12288)]
        vr = [at(b, D) for b in (W, W + 2048, Q + 2048, R + 2048)]
        F0 = Z + 448
        keysT = at(F0, 2048).rearrange("p (m n) -> p m n", m=16)
        dots, wts = (at(F0 + 2048 + 640 * i, 640) for i in range(2))
        idx = at(F0 + 3328, 640).bitcast(U32)
        F1 = F0 + 3968
        sh, sh2 = at(F1, 256), at(F1 + 256, 256)
        hv = at(F1 + 512, 32)
        hi = at(F1 + 544, 32).bitcast(U32)
        cv = at(F1 + 576, 16)
        ci = at(F1 + 592, 16).bitcast(U32)
        i12 = at(F1 + 608, 256).rearrange("p (c h k) -> p c h k", c=2, h=PH)
        topv = at(F1 + 864, 128).rearrange("p (h k) -> p h k", h=PH)
        topp = at(F1 + 992, 128).bitcast(U32)
        pos2 = at(F1 + 1120, 256)
        row = [at(F1 + 1376 + 128 * i, 128) for i in range(2)]
        hs8 = at(F1 + 1632, 8)
        stage = [at(F1 + 1640 + j, 1).bitcast(U32) for j in range(2 * RING)]
        bns = at(F1 + 1648, 24).rearrange("p (a b) -> p a b", a=4)
        bna = at(F1 + 1672, 2)
        lnr = at(F1 + 1674, 2)
        ident2 = at(F1 + 1704, P)
        cand, cand2 = (at(F1 + 1832 + 256 * i, 256) for i in range(2))
        diag = [at(F1 + 2344 + P * j, P) for j in range(4)]
        assert F1 + 2344 + 4 * P <= 53120

        uscr = nc.dram_tensor("u_scratch", [1024, SL, C], F32).ap()
        yscr = nc.dram_tensor("y_scratch", [1024, SL, C], F32).ap()
        kext = nc.dram_tensor("kernel_scratch", [GRP, SG, 15 * SG], F32).ap()
        tscr = nc.dram_tensor("toeplitz_scratch", [GP, P, 2, P], F32).ap()
        cscr = nc.dram_tensor("c_scratch", [GP, P, 2, 2, P], F32).ap()
        escr = nc.dram_tensor("distance_scratch", [H, EXT], F32).ap()
        mscr = nc.dram_tensor("bias_scratch", [H, P, BW], F32).ap()

        ssm_in, consts_in = sem("ssm_in"), sem("consts_in")
        x_in = sem("x_in")
        w_in = [sem(f"w_in{j}") for j in range(2)]
        slab_done = sem("slab_done")
        slab_out = sem("slab_out")
        u_stored, u_moved = sem("u_stored"), sem("u_moved")
        relb_in, ext_done, ext_stored, zero_done, zeros_stored, bias_done = (
            sem(n) for n in ("relb_in", "ext_done", "ext_stored", "zero_done", "zeros_stored", "bias_done"))
        mscr_made, h0_placed = sem("mscr_made"), sem("h0_placed")
        dtx, sq_r, trig = sem("dt_ready"), sem("angles_reduced"), sem("trig_done")
        tables = sem("ssm_tables")
        g_built, ca_built = sem("g_built"), sem("ca_built")
        ca_stored = [sem(f"ca_stored{j}") for j in range(2)]
        gtr, gt_ready, s_done = sem("g_transposed"), sem("gt_ready"), sem("s_done")
        k_done, ke_ready = sem("k_done"), sem("ke_ready")
        s_out, k_out = sem("s_out"), sem("k_out")
        ke_stored = [sem(f"ke_stored{j}") for j in range(2)]
        gtz_zero = sem("gtz_zero")
        h_ready = sem("h_ready")
        t_made = sem("t_made")
        y_in = [sem(f"y_in{j}") for j in range(4)]
        y_done, y_out = sem("y_done"), sem("y_out")
        y_stored, y_moved = sem("y_stored"), sem("y_moved")
        kv_out = sem("kv_out")
        outs = sem("outputs_stored")
        a_in = [sem(f"a_in{j}") for j in range(2)]
        pair_done = sem("pair_done")
        qz_ready, vs_ready, vt_done, vt_out = sem("qz_ready"), sem("vs_ready"), sem("vt_done"), sem("vt_out")
        sc_done, sc_used, mx_ready, ex_done, p_ready, pt_done, pt_out, o_done, o_out = (
            sem(n) for n in ("sc_done", "sc_used", "mx_ready", "ex_done", "p_ready", "pt_done", "pt_out",
                             "o_done", "o_out"))
        gw_ready, yd_ready, gelu_done, gate_done, sig_done, ssm_gated = (
            sem(n) for n in ("gw_ready", "yd_ready", "gelu_done", "gate_done", "sig_done", "ssm_gated"))
        sq_ready, sq_used, ms_done, rt_done, cat_ready = (
            sem(n) for n in ("sq_ready", "sq_used", "ms_done", "rt_done", "cat_ready"))
        ln_in, xt_in, xin_free, mt_done, res_ready, var_ready, sd_ready, nb_ready, xh_ready, x1_ready, x1t_done, x1t_out = (
            sem(n) for n in ("ln_in", "xt_in", "xin_free", "mt_done", "res_ready", "var_ready", "sd_ready",
                             "nb_ready", "xh_ready", "x1_ready", "x1t_done", "x1t_out"))
        keys_in, ln2_in = sem("keys_in"), sem("ln2_in")
        score_done, score_out, score_used = sem("score_done"), sem("score_out"), sem("score_used")
        gx, ge = sem("gate_logits"), sem("gate_exp")
        idx_ready = sem("idx_ready")
        u_got = [sem(f"u_got{j}") for j in range(RING)]
        v_got = [sem(f"v_got{j}") for j in range(RING)]
        u_used, v_used = sem("u_used"), sem("v_used")
        dots_ready, act_ready, wts_ready = sem("dots_ready"), sem("act_ready"), sem("wts_ready")
        diag_ready = sem("diag_ready")
        ffn_done, ffn_read = sem("ffn_done"), sem("ffn_read")
        var2, sd2, nb2, xh2, y_ready = sem("var2"), sem("sd2"), sem("nb2"), sem("xh2"), sem("y_ready")
        dve_chain, act_chain, pool_chain = sem("dve_chain"), sem("act_chain"), sem("pool_chain")

        NU = 10

        block = ctx.enter_context(nc.Block())

        @block.sync
        def _(sp):
            def slabs(first, count, src=None):
                src = first if src is None else src
                with sp.Fori(0, count // 2) as i:
                    for j in range(2):
                        sp.wait_ge(slab_done, first + 2 * i + j + 1)
                        sp.dma_start(wring[j].rearrange("p k c -> p (k c)"),
                                     a["w"][bass.ds(src + 2 * i + j, 1)].rearrange("a p n -> (a p) n")
                                     ).then_inc(w_in[j], 16)

            sp.dma_start(xT, a["x_t"].rearrange("(k p) t -> p k t", p=P)).then_inc(x_in, 16)
            slabs(0, 8)
            with sp.Fori(0, GP // 4) as i:
                for b in range(2):
                    sp.wait_ge(slab_done, 8 + 2 * i + b + 1)
                    sp.dma_start(wring[b].rearrange("p k c -> p (k c)"),
                                 a["w"][bass.ds(8 + 2 * i + b, 1)].rearrange("a p n -> (a p) n")
                                 ).then_inc(w_in[b], 16)
                    for q in range(2):
                        g = 4 * i + 2 * b + q
                        sp.wait_ge(ca_built, g + 1)
                        sp.dma_start(cscr[bass.ds(g, 1)].rearrange("a p r g n -> (a p) (r g) n"),
                                     CAz[q].rearrange("p r g n -> p (r g) n")[:, :, SG:NW * SG]
                                     ).then_inc(ca_stored[q], 16)
            slabs(24, 6)
            sp.wait_ge(slab_out, 26)
            sp.dma_start(o["k_t"].rearrange("(m p) t -> p m t", p=P),
                         qkv[:, 8 * T:16 * T].rearrange("p (m t) -> p m t", m=8)).then_inc(kv_out, 16)
            slabs(30, 2)
            sp.wait_ge(slab_done, 34)
            sp.wait_ge(mscr_made, 16)
            sp.wait_ge(h_ready, 1)
            sp.dma_start(o["h"], last.rearrange("p s r g -> p (s r g)")).then_inc(outs, 16)
            sp.wait_ge(slab_out, 34)
            sp.dma_start(o["v_t"].rearrange("(m p) t -> p m t", p=P),
                         qkv[:, 16 * T:24 * T].rearrange("p (m t) -> p m t", m=8)).then_inc(kv_out, 16)
            with sp.Fori(0, NPAIR // 2) as i:
                for b in range(2):
                    sp.wait_ge(pair_done, 2 * i + b + 1)
                    m = 2 * i + b
                    sp.dma_start(cK[b], a["ck"][bass.ds(m, 1)].rearrange("a p n -> (a p) n")).then_inc(a_in[b], 16)
                    sp.dma_start(cV[b].rearrange("p k n -> p (k n)"),
                                 a["cv"][bass.ds(m, 1)].rearrange("a p n -> (a p) n")).then_inc(a_in[b], 16)
                    sp.dma_start(Mb[b], mscr[bass.ds(2 * m, 2)].rearrange("h p c -> p h c")).then_inc(a_in[b], 16)
            slabs(32, 16)
            sp.wait_ge(cat_ready, 2)
            sp.dma_start(lng, a["ln1_g"].partition_broadcast(P)).then_inc(ln_in, 16)
            sp.dma_start(lnb, a["ln1_b"].partition_broadcast(P)).then_inc(ln_in, 16)

            def tokens(t):
                t0, n = TILES[t]
                for r0 in range(0, P, n):
                    sp.dma_start(xin[r0:r0 + n], a["x_tok"][t0:t0 + n, :]).then_inc(xt_in, 16)

            tokens(0)
            slabs(48, 16)
            sp.dma_start(keysT.rearrange("p m n -> p (m n)"), a["keys_t"]).then_inc(keys_in, 16)
            sp.dma_start(ident2, a["ident2"]).then_inc(keys_in, 16)
            slabs(64, 16, src=32)
            sp.wait_ge(u_used, FIRST + RING)
            for t in range(1, NT):
                sp.wait_ge(xin_free, t)
                tokens(t)
            slabs(80, 16, src=48)
            sp.wait_ge(x1_ready, NT)
            sp.dma_start(lng, a["ln2_g"].partition_broadcast(P)).then_inc(ln2_in, 16)
            sp.dma_start(lnb, a["ln2_b"].partition_broadcast(P)).then_inc(ln2_in, 16)
            for t, (t0, n) in enumerate(TILES):
                sp.wait_ge(y_ready, t + 1)
                sp.dma_start(o["y"][t0:t0 + n, :], x1[0:n, t, :]).then_inc(outs, 16)
            sp.wait_ge(outs, 16 * (NT + 1))
            sp.wait_ge(kv_out, 32)

        @block.gpsimd
        def _(pool):
            link = Chain(pool, pool_chain)
            pool.sem_inc(u_used, RING)
            pool.sem_inc(v_used, RING)
            pool.wait_ge(ext_done, 1)
            pool.dma_start(escr, ext).then_inc(ext_stored, 16)
            pool.wait_ge(zero_done, 1)
            pool.dma_start(kext.rearrange("(g a) h n -> (a h) g n", a=8)[:, :, 0:7 * SG],
                           zer.rearrange("p (g n) -> p g n", g=8)).then_inc(zeros_stored, 16)
            pool.wait_ge(ext_stored, 16)
            shifted = bass.AP(tensor=escr.tensor, offset=P - 1, ap=[[EXT, H], [-1, P], [1, BW]])
            pool.dma_start(mscr, shifted).then_inc(mscr_made, 16)
            pool.wait_ge(zeros_stored, 16)
            pool.sem_inc(bias_done, 1)
            link(nc.gpsimd.memset(CAz[0].rearrange("p r g n -> p (r g n)"), 0.0))
            link(nc.gpsimd.memset(CAz[1].rearrange("p r g n -> p (r g n)"), 0.0))
            pool.wait_ge(tables, 1)

            def ca_round(i):
                for b in range(2):
                    g = 2 * i + b
                    wv = lambda t: t[:, bass.ds(g, 1), :].rearrange("p a k -> p (a k)").unsqueeze(2).to_broadcast([P, NW, SG])
                    cvv = lambda t: t[:, bass.ds(g, 1), :].to_broadcast([P, NW, SG])
                    pool.wait_ge(k_done, g + 1)
                    if not (isinstance(i, int) and i == 0):
                        pool.wait_ge(ca_stored[b], 16 * i)
                    for r, (w1, c1, w2, c2) in enumerate(((Wr, Cr, NWi, Ci), (NWi, Cr, Wr, Ci))):
                        link(nc.gpsimd.tensor_tensor(tP[0], wv(w1), cvv(c1), ALU.mult))
                        link(nc.gpsimd.tensor_tensor(tP[1], wv(w2), cvv(c2), ALU.mult))
                        for g2 in range(2):
                            s = slice(64 * g2, 64 * g2 + 64)
                            dst = CAz[b][s, r, g2, :].rearrange("p (k h) -> p k h", k=NW)
                            link(nc.gpsimd.tensor_tensor(dst, tP[0][s], tP[1][s],
                                                         ALU.add if r == 0 else ALU.subtract))
                    pool.sem_inc(ca_built, 1)

            ca_round(0)
            link.zero()
            with pool.Fori(1, GP // 2) as i:
                ca_round(i)
                link.zero()
            for b in range(2):
                pool.wait_ge(ca_stored[b], 16 * (GP // 2))
                pool.wait_ge(ke_stored[b], 16 * (GP // 2) + 16)
            for k in range(SL):
                for g2 in range(2):
                    pool.dma_start(tscr.rearrange("a (k h) g n -> g k h a n", k=SL)[g2, k],
                                   kext.rearrange("(a g) h n -> g h a n", g=2)[g2, :, :, k * SG:k * SG + P]
                                   ).then_inc(t_made, 16)
            pool.wait_ge(slab_done, 34)
            pool.wait_ge(slab_out, 34)
            for b in range(2):
                link(nc.gpsimd.memset(qz[b].rearrange("p h t -> p (h t)"), 0.0))
            link.zero()
            with pool.Fori(0, NPAIR // 2) as i:
                for b in range(2):
                    m = 2 * i + b
                    pool.wait_ge(pair_done, m + 1)
                    for hh in range(2):
                        s = slice(64 * hh, 64 * hh + 64)
                        link(nc.gpsimd.tensor_copy(qz[b][s, hh, :], qkv[s, bass.ds(m * T, T)]))
                    pool.sem_inc(qz_ready, 1)
                    pool.wait_ge(vt_done, m + 1)
                    link(nc.gpsimd.tensor_copy(vs, qkv[:, bass.ds(16 * T + m * T, T)]))
                    pool.sem_inc(vs_ready, 1)
                link.zero()
            pool.wait_ge(y_stored, 16 * SL)
            pool.dma_start(yT, yscr.rearrange("(m p) s c -> p m (s c)", p=P)).then_inc(y_moved, 16)
            link.zero()
            table = {0: a["peer_u"], 1: a["peer_v"]}

            def fetch(kind, t, step, slot):
                ring, got = ((ur, u_got), (vr, v_got))[kind]
                s = stage[RING * kind + slot]
                link(nc.gpsimd.tensor_copy(s, idx[:, bass.ds(t * KK + step, 1)]))
                pool.indirect_dma_start(
                    out=ring[slot], out_offset=None, in_=table[kind],
                    in_offset=bass.IndirectOffsetOnAxis(ap=s, axis=0)).then_inc(got[slot], 16)

            def rows_of(tu, u0, nu, tv, v0, nv):
                turns = max(nu, nv) // 8
                with pool.Fori(0, turns) as i:
                    for j in range(8):
                        for kind, t, s0, per in ((0, tu, u0, nu // turns), (1, tv, v0, nv // turns)):
                            if per == 0 or j * per % 8:
                                continue
                            jj = j * per // 8
                            pool.wait_ge((u_used, v_used)[kind], t * KK + s0 + per * i + jj + 1)
                            fetch(kind, t, s0 + per * i + jj, jj % RING)
                    link.zero()

            pool.wait_ge(idx_ready, 1)
            rows_of(0, 0, FIRST - FIRST % 8, 0, 0, 0)
            for j in range(FIRST % 8):
                s0 = FIRST - FIRST % 8 + j
                pool.wait_ge(u_used, s0 + 1)
                fetch(0, 0, s0, j)
            link.zero()
            pool.wait_ge(u_used, FIRST + RING)
            with pool.Fori(0, DURING // 2) as i:
                for j in range(2):
                    pool.wait_ge(u_used, FIRST + 2 * i + j + RING - 1)
                    fetch(0, 0, FIRST + 2 * i + j, j)
                link.zero()
            pool.wait_ge(x1_ready, NT)
            pool.wait_ge(u_used, FIRST + DURING + RING)
            with pool.Fori(0, (KK - FIRST - DURING) // RING) as i:
                for j in range(RING):
                    step = FIRST + DURING + RING * i + j
                    pool.wait_ge(u_used, step + 1)
                    fetch(0, 0, step, j)
                link.zero()
            pool.wait_ge(score_out, 2)
            rows_of(0, 0, 0, 0, 0, LEAD)
            pool.wait_ge(idx_ready, 2)
            rows_of(1, 0, KK - LEAD, 0, LEAD, KK - LEAD)
            rows_of(1, KK - LEAD, LEAD, 0, 0, 0)
            for seg in range(2, NT + 1):
                if seg < NT:
                    pool.wait_ge(idx_ready, seg + 1)
                rows_of(seg, 0, STEPS[seg] if seg < NT else 0, seg - 1, 0, STEPS[seg - 1])

        @block.scalar
        def _(act):
            link = Chain(act, act_chain)
            act.sem_inc(slab_out, 2)
            act.sem_inc(pt_out, 2)
            act.sem_inc(gt_ready, 1)
            act.sem_inc(k_out, 1)
            act.sem_inc(s_out, 1)
            act.sem_inc(y_out, 4)
            act.sem_inc(vt_out, 1)
            act.sem_inc(o_out, 1)
            for name, dst in (("a_re", are), ("a_im", aim), ("log_dt", ldt), ("h0_re", h0r), ("h0_im", h0i)):
                act.dma_start(dst, a[name]).then_inc(ssm_in, 16)
            for name, dst in (("b_re", Br), ("b_im", Bi), ("c_re", Cr), ("c_im", Ci)):
                act.dma_start(dst, a[name].rearrange("p (g h) -> p g h", g=GP)).then_inc(ssm_in, 16)
            act.dma_start(relb, a["rel_bias"]).then_inc(relb_in, 16)
            for name, dst in (("ident", ident), ("block", blk), ("iota", iota), ("ssm_d", dvec), ("glu_b", glub),
                              ("g_attn", gA), ("g_ssm", gS)):
                act.dma_start(dst, a[name]).then_inc(consts_in, 16)
            act.dma_start(glw, a["glu_w"].rearrange("p (m k) -> p m k", m=8)).then_inc(consts_in, 16)
            act.wait_ge(ssm_in, 16 * 9)
            nc.scalar.activation(dt, ldt, ACT.Exp).then_inc(dtx, 1)
            act.wait_ge(sq_r, 1)
            nc.scalar.activation(er, ta, ACT.Exp).then_inc(trig, 1)
            act.wait_ge(sq_r, 2)
            nc.scalar.activation(sinv, rn, ACT.Sin).then_inc(trig, 1)
            nc.scalar.activation(cosv, tb, ACT.Sin).then_inc(trig, 1)

            def product(n, b, dst, perm, scale=1.0):
                act.wait_ge(slab_done, n + 3)
                if perm:
                    nc.scalar.copy(dst[:, :, 0:CP], bank[b][:, :].rearrange("p (c s) -> p s c", s=SL))
                    nc.scalar.copy(dst[:, :, CP:C], bank[2 + b][:, 0:TS].rearrange(
                        "p (c s) -> p s c", s=SL)).then_inc(slab_out, 1)
                else:
                    nc.scalar.activation(dst(0, TP), bank[b][:, :], ACT.Copy, scale=scale)
                    nc.scalar.activation(dst(TP, TS), bank[2 + b][:, 0:TS], ACT.Copy, scale=scale
                                         ).then_inc(slab_out, 1)

            with act.Fori(0, 4) as i:
                for b in range(2):
                    product(2 * i + b, b, uP[:, bass.ds(2 * i + b, 1)].rearrange("p m s c -> p (m s) c"), True)
            act.wait_ge(slab_out, 10)
            act.dma_start(uscr.rearrange("(m p) s c -> p m (s c)", p=P),
                          uP.rearrange("p m s c -> p m (s c)")).then_inc(u_stored, 16)
            act.wait_ge(u_stored, 16)
            for k in range(SL):
                act.dma_start(U8[k * SG:(k + 1) * SG],
                              uscr.rearrange("(g h) s c -> s h g c", h=SG)[SL - 1 - k]).then_inc(u_moved, 16)
            act.wait_ge(gtz_zero, 1)
            act.wait_ge(h0_placed, 1)

            for b in range(2):
                act.sem_inc(ke_stored[b], 16)
            act.wait_ge(bias_done, 1)
            for lo, hi_, scale in ((0, 4, DH ** -0.5), (4, 8, 1.0)):
                with act.Fori(lo, hi_) as i:
                    for b in range(2):
                        for q in range(2):
                            g = 4 * i + 2 * b + q
                            act.wait_ge(gtr, g + 1)
                            act.wait_ge(s_done, g + 1)
                            for g2 in range(2):
                                c = slice(64 * g2, 64 * g2 + 64)
                                ins = nc.scalar.copy(GTz[q][:, :, g2, c], gtp[q].rearrange(
                                    "p (r n) -> p r n", r=2)[:, :, c])
                            ins.then_inc(gt_ready, 1)
                        n = 2 * i + b
                        product(8 + n, b, lambda o_, w_: qkv[:, bass.ds(n * T + o_, w_)], False, scale)
                        for q in range(2):
                            g = 4 * i + 2 * b + q
                            act.wait_ge(k_done, g + 3)
                            act.wait_ge(ke_stored[q], 32 * i + 16 * b + 16)
                            nc.scalar.copy(KE[q], acc[0:SG, 0:256]).then_inc(k_out, 1)
                            act.wait_ge(s_done, g + 3)
                            hview = Hs[:, :, bass.ds(g, 1), :].rearrange("p r g c -> p (r g) c")
                            sview = acc[:, 512:512 + 2 * C].rearrange("p (r c) -> p r c", r=2)
                            nc.scalar.copy(hview[:, :, 1:CP + 1], sview[:, :, 0:CP])
                            nc.scalar.copy(hview[:, :, CP + 2:SLOTS], sview[:, :, CP:C]).then_inc(s_out, 1)
                            act.wait_ge(k_out, g + 2)
                            act.dma_start(kext[bass.ds(2 * g, 2)].rearrange("g h n -> h g n")[:, :, 7 * SG:15 * SG],
                                          KE[q].rearrange("p (g n) -> p g n", g=2)).then_inc(ke_stored[q], 16)
            with act.Fori(8, 12) as i:
                for b in range(2):
                    n = 2 * i + b
                    product(8 + n, b, lambda o_, w_: qkv[:, bass.ds(n * T + o_, w_)], False)
            act.wait_ge(slab_out, 34)
            act.wait_ge(t_made, 32 * SL)

            def y_load(b, g):
                act.dma_start(Tt[b].rearrange("p g n -> p (g n)"),
                              tscr[g].rearrange("a p g n -> (a p) (g n)")).then_inc(y_in[b], 16)
                act.dma_start(CAy[b].rearrange("p r g n -> p (r g n)"),
                              cscr[g].rearrange("a p r g n -> (a p) (r g n)")).then_inc(y_in[b], 16)

            for b in range(4):
                y_load(b, slice(b, b + 1))
            with act.Fori(0, GP // 4 - 1) as i:
                for b in range(4):
                    g = 4 * i + b
                    act.wait_ge(y_done, g + 1)
                    nc.scalar.copy(U8[:, bass.ds(2 * g, 2), :].rearrange("p g c -> p (g c)"),
                                   bank[b][:, 0:2 * C]).then_inc(y_out, 1)
                    y_load(b, bass.ds(g + 4, 1))
            for b in range(4):
                g = GP - 4 + b
                act.wait_ge(y_done, g + 1)
                nc.scalar.copy(U8[:, 2 * g:2 * g + 2, :].rearrange("p g c -> p (g c)"),
                               bank[b][:, 0:2 * C]).then_inc(y_out, 1)
            act.wait_ge(y_out, GP + 4)
            for t in range(SL):
                act.dma_start(yscr.rearrange("(g h) s c -> s h g c", h=SG)[t],
                              U8[t * SG:(t + 1) * SG]).then_inc(y_stored, 16)
            with act.Fori(0, NPAIR // 2) as i:
                for b in range(2):
                    m = 2 * i + b

                    def exp(u):
                        rows = TS if u % 5 == 4 else P
                        keys = T if u % 5 == 4 else P * (u % 5 + 1)
                        act.wait_ge(mx_ready, m * NU + u + 1)
                        nc.scalar.activation(St[u % 2][0:rows, 0:keys], St[u % 2][0:rows, 0:keys], ACT.Exp,
                                             bias=st[u % 2][0:rows, 1:2], accum_out=st[u % 2][0:rows, 2:3]
                                             ).then_inc(ex_done, 1)

                    act.wait_ge(vt_done, m + 2)
                    act.wait_ge(pair_done, m + 1)
                    nc.scalar.copy(Vs[b][:, 0:4, :].rearrange("p k n -> p (k n)"), acc[:, 1024:1536])
                    nc.scalar.copy(Vs[b][0:TS, 4, :], acc[0:TS, 512:640]).then_inc(vt_out, 1)
                    exp(0)
                    for u in range(NU):
                        if u + 1 < NU:
                            exp(u + 1)
                        act.wait_ge(pt_done, m * NU + u + 3)
                        act.wait_ge(o_done, m * NU + u + 1)
                        src = acc[:, 512 * (u % 2):512 * (u % 2) + 512]
                        if u % 5 < 4:
                            n = u % 5 + 1
                            ins = nc.scalar.copy(PT[u % 2][:, 0:n, :].rearrange("p k n -> p (k n)"), src[:, 0:n * P])
                        else:
                            nc.scalar.copy(PT[u % 2][:, 0:4, 0:TS],
                                           src[:, 0:4 * TS].rearrange("p (k n) -> p k n", k=4))
                            ins = nc.scalar.copy(PT[u % 2][0:TS, 4, 0:TS], src[0:TS, 256:256 + TS])
                        ins.then_inc(pt_out, 1)
                    act.wait_ge(o_done, m * NU + NU + 2)
                    nc.scalar.copy(qkv[:, bass.ds(m * T, TP)], acc[:, 1536:2048])
                    nc.scalar.copy(qkv[:, bass.ds(m * T + TP, TS)], bank[3][:, 0:TS]).then_inc(o_out, 1)
            act.wait_ge(consts_in, 16 * 8)
            for m in range(8):
                act.wait_ge(yd_ready, m + 1)
                nc.scalar.activation(yT[:, m, :], yT[:, m, :], ACT.Gelu).then_inc(gelu_done, 1)
            for m in range(8):
                act.wait_ge(gate_done, m + 1)
                if m >= 2:
                    act.wait_ge(ssm_gated, m - 1)
                nc.scalar.activation(gt[m % 2][:, 0:TP], bank[m % 2][:, :], ACT.Sigmoid, bias=glub[:, m:m + 1])
                nc.scalar.activation(gt[m % 2][:, TP:T], bank[2 + m % 2][:, 0:TS], ACT.Sigmoid,
                                     bias=glub[:, m:m + 1]).then_inc(sig_done, 1)
            act.wait_ge(o_out, NPAIR + 1)
            for n in range(16):
                src = attT[:, n, :] if n < 8 else yT[:, n - 8, :]
                if n >= 8:
                    act.wait_ge(ssm_gated, n - 7)
                if n >= 2:
                    act.wait_ge(sq_used, n - 1)
                nc.scalar.activation(sq[n % 2], src, ACT.Square).then_inc(sq_ready, 1)
            for n in range(2):
                act.wait_ge(ms_done, n + 1)
                nc.scalar.activation(rs[n][:, 0:TP], bank[n][:, :], ACT.Sqrt, bias=eps_rms, scale=1.0 / 1024)
                nc.scalar.activation(rs[n][:, TP:T], bank[2 + n][:, 0:TS], ACT.Sqrt, bias=eps_rms,
                                     scale=1.0 / 1024).then_inc(rt_done, 1)
            act.wait_ge(kv_out, 32)
            def mixed(first, group):
                c0, width = GROUPS[group]
                with act.Fori(0, 8) as i:
                    for b in range(2):
                        act.wait_ge(slab_done, first + 2 * i + b + 3)
                        nc.scalar.copy(at(K, KT * T)[:, bass.ds((2 * i + b) * T + c0, width)],
                                       bank[b][:, 0:width]).then_inc(slab_out, 1)

            def ln1(t):
                n = TILES[t][1]
                t0 = TILES[t][0]
                act.wait_ge(var_ready, t + 1)
                nc.scalar.activation(lnr[:, 0:1], bna[:, 1:2], ACT.Sqrt, bias=eps_ln).then_inc(sd_ready, 1)
                act.wait_ge(nb_ready, t + 1)
                nc.scalar.activation(xhat, xhat, ACT.Identity, bias=lnr[:, 1:2], scale=lnr[:, 0:1]).then_inc(xh_ready, 1)
                for c in range(4):
                    act.wait_ge(x1t_done, 4 * t + c + 1)
                    for q in range(4):
                        f = 4 * c + q
                        dst = (attT if f < 8 else yT)[:, f % 8, t0:t0 + n]
                        ins = nc.scalar.copy(dst, bank[c % 2][:, P * q:P * q + n])
                    ins.then_inc(x1t_out, 1)
            def scores(t):
                for c in range(4):
                    act.wait_ge(score_done, 4 * t + c + 1)
                    if t and c == 0:
                        act.wait_ge(score_used, t)
                    ins = nc.scalar.copy(scored(t)[:, 512 * c:512 * c + 512], bank[c][:, :])
                ins.then_inc(score_out, 1)

            def gates(t):
                act.wait_ge(gx, t + 1)
                nc.scalar.activation(row[0], row[0], ACT.Exp).then_inc(ge, 1)

            def diags(t, k0, k1):
                src = ident if TILES[t][1] == P else ident2
                with act.Fori(k0 // 4, k1 // 4) as i:
                    for j in range(4):
                        act.wait_ge(v_used, t * KK + 4 * i + j + 1)
                        nc.scalar.activation(diag[j], src, ACT.Copy,
                                             scale=wts[:, bass.ds(t * KK + 4 * i + j, 1)]).then_inc(diag_ready, 1)

            mixed(32, 0)
            ln1(0)
            mixed(48, 0)
            scores(0)
            mixed(64, 1)
            gates(0)
            for t in range(1, NT):
                ln1(t)
            mixed(80, 1)
            scores(1)
            for seg in range(NT + 1):
                if seg:
                    act.wait_ge(wts_ready, seg)
                first = LEAD if seg == 1 else 0
                half = STEPS[seg - 1] // 2 + (LEAD + 8 if seg == 1 else 0)
                if seg == 1:
                    diags(0, 0, LEAD)
                    gates(1)
                if seg and seg + 1 < NT:
                    scores(seg + 1)
                if seg:
                    diags(seg - 1, first, half)
                if seg and seg + 1 < NT:
                    gates(seg + 1)
                if seg:
                    diags(seg - 1, half, STEPS[seg - 1])
                if seg < NT:
                    n = STEPS[seg]
                    act.wait_ge(dots_ready, seg + 1)
                    nc.scalar.activation(row[1][:, 0:n], dots[:, seg * KK:seg * KK + n], ACT.Gelu).then_inc(act_ready, 1)
                if seg:
                    act.wait_ge(var2, seg)
                    nc.scalar.activation(lnr[:, 0:1], bna[:, 1:2], ACT.Sqrt, bias=eps_ln).then_inc(sd2, 1)
                    act.wait_ge(nb2, seg)
                    nc.scalar.activation(x1[:, seg - 1, :], x1[:, seg - 1, :], ACT.Identity, bias=lnr[:, 1:2],
                                         scale=lnr[:, 0:1]).then_inc(xh2, 1)

        @block.vector
        def _(dve):
            link = Chain(dve, dve_chain)
            tt, ts_, stt = nc.vector.tensor_tensor, nc.vector.tensor_scalar, nc.vector.scalar_tensor_tensor
            dve.sem_inc(sc_used, 2)
            nc.vector.memset(zer, 0.0).then_inc(zero_done, 1)
            for b in range(2):
                ins = nc.vector.memset(GTz[b].rearrange("p r g n -> p (r g n)"), 0.0)
            ins.then_inc(gtz_zero, 1)
            nc.vector.memset(eps_ln, LN_EPS)
            nc.vector.memset(eps_rms, RMS_EPS)
            link(nc.vector.memset(ones, 1.0))
            dve.wait_ge(relb_in, 16)
            link(nc.vector.tensor_copy(ext[:, 0:511], relb[:, 0:1].to_broadcast([H, 511])))
            nc.vector.tensor_copy(ext[:, 511:EXT], relb).then_inc(ext_done, 1)
            dve.wait_ge(dtx, 1)
            tt(ta, are, dt, ALU.mult).then_inc(sq_r, 1)
            link(tt(th, aim, dt, ALU.mult))
            link(ts_(nr, th, 1.0 / (2 * math.pi), MAGIC, ALU.mult, ALU.add))
            link(ts_(nr, nr, -MAGIC, None, ALU.add))
            for c in (C1, C2, C3):
                link(stt(th, nr, -c, th, ALU.mult, ALU.add))
            link(ts_(rn, th, PI_IN, -PI_IN, ALU.min, ALU.max))
            link(ts_(tb, rn, -1.0, None, ALU.mult))
            link(tt(tb, tb, rn, ALU.max))
            ts_(tb, tb, -1.0, math.pi / 2, ALU.mult, ALU.add).then_inc(sq_r, 1)
            dve.wait_ge(trig, 3)
            w = lambda t, k: t[:, :, k]
            link(nc.vector.memset(w(Wr, 0), 1.0))
            link(nc.vector.memset(w(Wi, 0), 0.0))
            link(tt(w(Wr, 1), er, cosv, ALU.mult))
            link(tt(w(Wi, 1), er, sinv, ALU.mult))
            link(ts_(nr, w(Wr, 1), -1.0, None, ALU.add))
            link(tt(ta, are, are, ALU.mult))
            link(tt(tb, aim, aim, ALU.mult))
            link(tt(den, ta, tb, ALU.add))
            link(nc.vector.reciprocal(den, den))
            link(tt(ta, nr, are, ALU.mult))
            link(tt(tb, w(Wi, 1), aim, ALU.mult))
            link(tt(ta, ta, tb, ALU.add))
            link(tt(fr, ta, den, ALU.mult))
            link(tt(ta, w(Wi, 1), are, ALU.mult))
            link(tt(tb, nr, aim, ALU.mult))
            link(tt(ta, ta, tb, ALU.subtract))
            link(tt(fi, ta, den, ALU.mult))
            bch = lambda t: t.unsqueeze(2).to_broadcast([P, GP, SG])
            tm = [at(Q + 512 * i, 512).rearrange("p (g h) -> p g h", g=GP) for i in range(4)]
            link(tt(tm[0], Br, bch(fr), ALU.mult))
            link(tt(tm[1], Bi, bch(fi), ALU.mult))
            link(tt(tm[2], Bi, bch(fr), ALU.mult))
            link(tt(tm[3], Br, bch(fi), ALU.mult))
            link(tt(Br, tm[0], tm[1], ALU.subtract))
            link(tt(Bi, tm[2], tm[3], ALU.add))
            for k in range(1, SL):
                link(tt(ta, w(Wr, k), w(Wr, 1), ALU.mult))
                link(tt(tb, w(Wi, k), w(Wi, 1), ALU.mult))
                link(tt(w(Wr, k + 1), ta, tb, ALU.subtract))
                link(tt(ta, w(Wr, k), w(Wi, 1), ALU.mult))
                link(tt(tb, w(Wi, k), w(Wr, 1), ALU.mult))
                link(tt(w(Wi, k + 1), ta, tb, ALU.add))
            link(ts_(NWi, Wi, -1.0, None, ALU.mult))
            link(nc.vector.memset(Hs[:, :, :, 0], 0.0))
            link(nc.vector.tensor_copy(Hs[:, 0, :, CP + 1], h0r))
            link(nc.vector.tensor_copy(Hs[:, 1, :, CP + 1], h0i))
            dve.sem_inc(h0_placed, 1)
            dve.sem_inc(tables, 1)
            link.zero()
            with dve.Fori(0, GP // 2) as i:
                for b in range(2):
                    g = 2 * i + b
                    wv = lambda t: t[:, bass.ds(g, 1), 0:SL].rearrange("p a k -> p (a k)").unsqueeze(2).to_broadcast([P, SL, SG])
                    bv = lambda t: t[:, bass.ds(g, 1), :].to_broadcast([P, SL, SG])
                    dve.wait_ge(k_done, g + 1)
                    link(tt(tD[0], wv(Wr), bv(Br), ALU.mult))
                    link(tt(tD[1], wv(Wi), bv(Bi), ALU.mult))
                    link(tt(Gb[b][:, 0], tD[0], tD[1], ALU.subtract))
                    link(tt(tD[0], wv(Wr), bv(Bi), ALU.mult))
                    link(tt(tD[1], wv(Wi), bv(Br), ALU.mult))
                    link(tt(Gb[b][:, 1], tD[0], tD[1], ALU.add))
                    dve.sem_inc(g_built, 1)
                link.zero()
            dve.wait_ge(s_out, GP + 1)
            for c0, cn in ((0, CP), (CP + 1, CS)):
                link.zero()
                with dve.Fori(0, cn) as i:
                    h = Hs[:, :, :, bass.ds(c0 + i, 1)].rearrange("p r g c -> p r (g c)")
                    nxt = Hs[:, :, :, bass.ds(c0 + 1 + i, 1)].rearrange("p r g c -> p r (g c)")
                    w8 = lambda t: t[:, :, SL].unsqueeze(1).to_broadcast([P, 2, GP])
                    link(tt(scP, h, w8(Wr), ALU.mult))
                    link(tt(scQ, h, w8(Wi), ALU.mult))
                    link(tt(scP, scP, nxt, ALU.add))
                    link(tt(nxt[:, 0], scP[:, 0], scQ[:, 1], ALU.subtract))
                    link(tt(nxt[:, 1], scP[:, 1], scQ[:, 0], ALU.add))
                    link.zero()
            link(nc.vector.tensor_copy(last[:, 0], Hs[:, :, :, CP]))
            link(nc.vector.tensor_copy(last[:, 1], Hs[:, :, :, SLOTS - 1]))
            hm = at(E0, 2 * GP * CS).rearrange("p (r g c) -> p r g c", r=2, g=GP)
            link(nc.vector.tensor_copy(hm[:, 0], Hs[:, 0, :, CP + 1:CP + 1 + CS]))
            link(nc.vector.tensor_copy(hm[:, 1], Hs[:, 1, :, CP + 1:CP + 1 + CS]))
            link(nc.vector.tensor_copy(Hs[:, 0, :, CP:C], hm[:, 0]))
            link(nc.vector.tensor_copy(Hs[:, 1, :, CP:C], hm[:, 1]))
            dve.sem_inc(h_ready, 1)
            link.zero()
            with dve.Fori(0, NPAIR // 2) as i:
                for b in range(2):
                    m = 2 * i + b
                    dve.wait_ge(a_in[b], 48 * i + 48)
                    link(nc.vector.memset(Mb[b][0:CH, :, BW - CH:BW], NEG))

                    def front(u):
                        hh, j = divmod(u, 5)
                        rows, keys = (P, P * (j + 1)) if j < 4 else (TS, T)
                        S, stat = St[u % 2][0:rows], st[u % 2][0:rows]
                        dve.wait_ge(sc_done, m * NU + u + 1)
                        dve.wait_ge(pt_done, m * NU + u + 1)
                        if j < 4:
                            link(tt(S[:, 0:keys], bank[u % 2][:, 0:keys], Mb[b][:, hh, TP - P * j:BW], ALU.add))
                        else:
                            tt(S[:, 0:TP], bank[u % 2][0:TS, :], Mb[b][0:TS, hh, 0:TP], ALU.add)
                            link(tt(S[:, TP:T], bank[2][0:TS, 0:TS], Mb[b][0:TS, hh, TP:T], ALU.add))
                        dve.sem_inc(sc_used, 1)
                        link(nc.vector.reduce_max(stat[:, 0:1], S[:, 0:keys], AX.X))
                        ts_(stat[:, 1:2], stat[:, 0:1], -1.0, None, ALU.mult).then_inc(mx_ready, 1)

                    def back(u):
                        j = u % 5
                        rows, keys = (P, P * (j + 1)) if j < 4 else (TS, T)
                        S, stat = St[u % 2][0:rows], st[u % 2][0:rows]
                        dve.wait_ge(ex_done, m * NU + u + 1)
                        link(nc.vector.reciprocal(stat[:, 3:4], stat[:, 2:3]))
                        ts_(S[:, 0:keys], S[:, 0:keys], stat[:, 3:4], None, ALU.mult).then_inc(p_ready, 1)

                    front(0)
                    for u in range(NU):
                        if u + 1 < NU:
                            front(u + 1)
                        back(u)
                link.zero()
            dve.wait_ge(consts_in, 16 * 8)
            for m in range(8):
                ins = tt(GW[:, m, :].rearrange("p (g k) -> p g k", g=8),
                         glw[:, m, :].unsqueeze(1).to_broadcast([P, 8, SG]),
                         blk.rearrange("p (g k) -> p g k", g=8), ALU.mult)
            ins.then_inc(gw_ready, 1)
            dve.wait_ge(y_moved, 16)
            for m in range(8):
                stt(yT[:, m, :], uP[:, m].rearrange("p s c -> p (s c)"), dvec[:, m:m + 1], yT[:, m, :],
                    ALU.mult, ALU.add).then_inc(yd_ready, 1)
            for m in range(8):
                dve.wait_ge(sig_done, m + 1)
                tt(yT[:, m, :], yT[:, m, :], gt[m % 2], ALU.mult).then_inc(ssm_gated, 1)
            for n in range(2):
                dve.wait_ge(rt_done, n + 1)
                link(nc.vector.reciprocal(rs[n], rs[n]))
                for m in range(8):
                    if n == 0:
                        ins = stt(attT[:, m, :], attT[:, m, :], gA[:, m:m + 1], rs[0], ALU.mult, ALU.mult)
                    else:
                        tmp = gt[m % 2]
                        link(stt(tmp, yT[:, m, :], gS[:, m:m + 1], rs[1], ALU.mult, ALU.mult))
                        v = tmp.rearrange("p (s c) -> p s c", s=SL)
                        nc.vector.tensor_copy(yT[:, m, 0:TP].rearrange("p (c s) -> p s c", s=SL), v[:, :, 0:CP])
                        ins = nc.vector.tensor_copy(yT[:, m, TP:T].rearrange("p (c s) -> p s c", s=SL), v[:, :, CP:C])
                        if m < 7:
                            link(ins)
                ins.then_inc(cat_ready, 1)

            def norm(xv, var, sd, nb, xh, ready, t):
                for c in range(4):
                    ins = nc.vector.bn_stats(bns[:, c, :], xv[:, 512 * c:512 * c + 512])
                link(ins)
                nc.vector.bn_aggr(bna, bns.rearrange("p a b -> p (a b)")).then_inc(var, 1)
                dve.wait_ge(sd, t + 1)
                link(nc.vector.reciprocal(lnr[:, 0:1], lnr[:, 0:1]))
                stt(lnr[:, 1:2], bna[:, 0:1], -1.0, lnr[:, 0:1], ALU.mult, ALU.mult).then_inc(nb, 1)
                dve.wait_ge(xh, t + 1)

            dve.wait_ge(ln_in, 32)
            def ln1(t):
                n = TILES[t][1]
                dve.wait_ge(xt_in, 16 * (t + 1 if n == P else t + 2))
                dve.wait_ge(mt_done, t + 1)
                ins = stt(xhat, xin, ALPHA, acc[:, :], ALU.mult, ALU.add)
                ins.then_inc(res_ready, 1)
                dve.wait_ge(res_ready, t + 1)
                dve.sem_inc(xin_free, 1)
                norm(xhat, var_ready, sd_ready, nb_ready, xh_ready, x1_ready, t)
                link(tt(xhat, xhat, lng, ALU.mult))
                tt(x1[:, t, :], xhat, lnb, ALU.add).then_inc(x1_ready, 1)

            def head(t, h):
                s, s2 = sh, sh2
                link(nc.vector.tensor_copy(s, scored(t)[:, bass.ds(h * 256, 256)]))
                for c in range(2):
                    v, ix = hv[:, 16 * c:16 * c + 16], hi[:, 16 * c:16 * c + 16]
                    sc_, sc2 = s[:, P * c:P * c + P], s2[:, P * c:P * c + P]
                    top16(v, ix, sc_, sc2)
                cd = cand.rearrange("p (a b) -> p a b", a=TOPK)
                link(tt(cd, hv[:, 0:16].unsqueeze(2).to_broadcast([P, TOPK, TOPK]),
                        hv[:, 16:32].unsqueeze(1).to_broadcast([P, TOPK, TOPK]), ALU.add))
                top16(cv, ci, cand, cand2)
                for c in range(2):
                    link(nc.vector.tensor_copy(i12[:, c, bass.ds(h, 1), :].rearrange("p h k -> p (h k)"),
                                               hi[:, 16 * c:16 * c + 16]))
                link(nc.vector.tensor_copy(topv[:, bass.ds(h, 1), :].rearrange("p h k -> p (h k)"), cv))
                link(nc.vector.tensor_copy(topp[:, bass.ds(h * 16, 16)], ci))

            def top16(v, ix, x, x2):
                link(nc.vector.max(v[:, 0:8], x))
                link(nc.vector.max_index(ix[:, 0:8], v[:, 0:8], x))
                link(nc.vector.match_replace(x2, v[:, 0:8], x, LOWEST))
                link(nc.vector.max(v[:, 8:16], x2))
                link(nc.vector.max_index(ix[:, 8:16], v[:, 8:16], x2))
            HEAD = 1 + 15 + 1 + 4

            def decode(t):
                dve.sem_inc(score_used, 1)
                pu = pos2.bitcast(U32)
                link(nc.vector.tensor_scalar(pu[:, 0:KK], topp, 4, None, ALU.logical_shift_right))
                link(nc.vector.tensor_scalar(pu[:, KK:2 * KK], topp, 15, None, ALU.bitwise_and))
                link(nc.vector.tensor_copy(pos2, pu))
                full = [P, PH, TOPK, TOPK]
                eq = onehot(t)
                e4 = eq.rearrange("p (h k j) -> p h k j", h=PH, k=TOPK)
                for c in range(2):
                    pc = pos2[:, KK * c:KK * c + KK].rearrange("p (h k) -> p h k", h=PH)
                    link(tt(e4, pc.unsqueeze(3).to_broadcast(full),
                            iota.unsqueeze(1).unsqueeze(1).to_broadcast(full), ALU.is_equal))
                    link(tt(e4, e4, i12[:, c].unsqueeze(2).to_broadcast(full), ALU.mult))
                    link(nc.vector.reduce_sum(row[c], eq.rearrange("p (k j) -> p k j", j=TOPK), AX.X))
                link(stt(idx[:, t * KK:(t + 1) * KK], row[0], float(NKEY), row[1], ALU.mult, ALU.add))
                if STEPS[t] < KK:
                    link(nc.vector.tensor_copy(idx[TS:P, t * KK:t * KK + STEPS[t]],
                                               idx[TS:P, t * KK + STEPS[t]:(t + 1) * KK]))
                dve.sem_inc(idx_ready, 1)
                rv = row[0].rearrange("p (h k) -> p h k", h=PH)
                tt(rv, topv, topv[:, :, 0:1].to_broadcast([P, PH, TOPK]), ALU.subtract).then_inc(gx, 1)

            def gate(t):
                rv = row[0].rearrange("p (h k) -> p h k", h=PH)
                dve.wait_ge(ge, t + 1)
                link(nc.vector.reduce_sum(hs8, rv, AX.X))
                link(nc.vector.reciprocal(hs8, hs8))
                link(tt(wts[:, t * KK:(t + 1) * KK].rearrange("p (h k) -> p h k", h=PH), rv,
                        hs8.unsqueeze(2).to_broadcast([P, PH, TOPK]), ALU.mult))
                if STEPS[t] < KK:
                    link(nc.vector.tensor_copy(wts[TS:P, t * KK:t * KK + STEPS[t]],
                                               wts[TS:P, t * KK + STEPS[t]:(t + 1) * KK]))

            def dot(t, i4, j):
                before = t * (KK // RING) + (DURING // 4 if j < 2 else -(DURING // 4))
                dve.wait_ge(u_got[j], 16 * (before + i4 + 1))
                stt(ur[j], ur[j], 1.0, x1[:, t, :], ALU.mult, ALU.mult,
                    accum_out=dots[:, bass.ds(t * KK + RING * i4 + j, 1)]).then_inc(u_used, 1)

            def dots0(lo, hi_, slots):
                with dve.Fori(0, (hi_ - lo) // slots) as i:
                    for j in range(slots):
                        step = lo + slots * i + j
                        if slots == 2:
                            count = FIRST // RING + (lo - FIRST) // 2 + i + 1
                        elif lo:
                            count = FIRST // RING + (DURING // 2 if j < 2 else 0) + i + 1
                        else:
                            count = i + 1
                        dve.wait_ge(u_got[j], 16 * count)
                        stt(ur[j], ur[j], 1.0, x1[:, 0, :], ALU.mult, ALU.mult,
                            accum_out=dots[:, bass.ds(step, 1)]).then_inc(u_used, 1)

            ln1(0)
            dve.wait_ge(score_out, 1)
            link.zero()
            with dve.Fori(0, PH) as h:
                head(0, h)
                link.zero()
            decode(0)
            dots0(0, FIRST, RING)
            gate(0)
            dve.wait_ge(u_used, FIRST + RING)
            for t in range(1, NT):
                ln1(t)
                dots0(FIRST + 2 * t - 2, FIRST + 2 * t, 2)
            for seg in range(NT + 1):
                if seg < NT:
                    more = seg + 1 < NT
                    link.zero()
                    if seg == 0:
                        dots0(FIRST + DURING, KK, RING)
                    else:
                        if more:
                            dve.wait_ge(score_out, seg + 2)
                        with dve.Fori(0, PH) as h:
                            if more:
                                head(seg + 1, h)
                            for q in range(2):
                                for j in range(RING):
                                    dot(seg, 2 * h + q, j)
                            if more:
                                link.zero()
                        if more:
                            decode(seg + 1)
                            gate(seg + 1)
                        if STEPS[seg] == KK:
                            with dve.Fori(16, 32) as i:
                                for j in range(RING):
                                    dot(seg, i, j)
                    n = STEPS[seg]
                    dve.wait_ge(u_used, seg * KK + n + RING)
                    dve.sem_inc(dots_ready, 1)
                    dve.wait_ge(act_ready, seg + 1)
                    wv_ = wts[:, seg * KK:seg * KK + n]
                    link(tt(wv_, wv_, row[1][:, 0:n], ALU.mult))
                    dve.sem_inc(wts_ready, 1)
                    if seg == 0:
                        dve.wait_ge(score_out, 2)
                        link.zero()
                        with dve.Fori(0, PH) as h:
                            head(1, h)
                            link.zero()
                        decode(1)
                        gate(1)
                if seg:
                    t = seg - 1
                    if t == 0:
                        dve.wait_ge(ln2_in, 32)
                    dve.wait_ge(ffn_done, seg)
                    xv = x1[:, t, :]
                    link(stt(xv, xv, ALPHA, acc[:, :], ALU.mult, ALU.add))
                    dve.sem_inc(ffn_read, 1)
                    norm(xv, var2, sd2, nb2, xh2, y_ready, t)
                    link(tt(xv, xv, lng, ALU.mult))
                    tt(xv, xv, lnb, ALU.add).then_inc(y_ready, 1)

        @block.tensor
        def _(pe):
            mm = nc.tensor.matmul

            def carrier():
                mm(bank[2][:, 400:402], ident, ident[:, 0:2], start=True, stop=True)

            pe.sem_inc(slab_done, 2)
            pe.sem_inc(k_done, 2)
            pe.sem_inc(s_done, 2)
            pe.sem_inc(pair_done, 2)
            pe.sem_inc(vt_done, 1)
            pe.sem_inc(pt_done, 2)
            pe.sem_inc(o_done, 2)
            pe.wait_ge(x_in, 16)

            def slab(first, i, b, rhs):
                pe.wait_ge(w_in[b], 16 * (first // 2 + 1 + i))
                pe.wait_ge(slab_out, first + 2 * i + b + 1)
                for k in range(KT):
                    mm(bank[b][:, :], wring[b][:, k, :], rhs(k)[:, 0:TP], start=k == 0, stop=k == KT - 1)
                    ins = mm(bank[2 + b][:, 0:TS], wring[b][:, k, :], rhs(k)[:, TP:T],
                             start=k == 0, stop=k == KT - 1)
                ins.then_inc(slab_done, 1)

            def gemm(first, count, rhs):
                with pe.Fori(0, count // 2) as i:
                    for b in range(2):
                        slab(first, i, b, rhs)

            xcols = lambda k: xT[:, k, :]
            gemm(0, 8, xcols)
            pe.wait_ge(consts_in, 16 * 8)
            with pe.Fori(0, GP // 4) as i:
                for b in range(2):
                    for q in range(2):
                        g = 4 * i + 2 * b + q
                        pe.wait_ge(g_built, g + 1)
                        pe.wait_ge(gt_ready, g + 1)
                        for r in range(2):
                            ins = nc.tensor.transpose(gtp[q][:, P * r:P * r + P],
                                                      Gb[q][:, r].rearrange("p k h -> p (k h)"), ident)
                        ins.then_inc(gtr, 1)
                    slab(8, i, b, xcols)
                    pe.wait_ge(u_moved, 16 * SL)
                    for q in range(2):
                        g = 4 * i + 2 * b + q
                        pe.wait_ge(ca_built, g + 1)
                        pe.wait_ge(k_out, g + 1)
                        for r in range(2):
                            ins = mm(acc[0:SG, 0:256].rearrange("p (g n) -> p g n", g=2), Gb[q][:, r, 0, :],
                                     CAz[q][:, r, :, 0:P], start=r == 0, stop=r == 1)
                        ins.then_inc(k_done, 1)
                        pe.wait_ge(gt_ready, g + 2)
                        pe.wait_ge(s_out, g + 1)
                        for r in range(2):
                            for g2 in range(2):
                                ins = mm(acc[:, 512 + C * r:512 + C * r + C], GTz[q][:, r, g2, :],
                                         U8[:, bass.ds(2 * g + g2, 1), :].rearrange("p g c -> p (g c)"),
                                         start=g2 == 0, stop=g2 == 1)
                        ins.then_inc(s_done, 1)
            gemm(24, 8, xcols)
            pe.wait_ge(h_ready, 1)
            with pe.Fori(0, GP // 4) as i:
                for b in range(4):
                    g = 4 * i + b
                    pe.wait_ge(y_in[b], 32 * i + 32)
                    pe.wait_ge(y_out, g + 1)
                    for g2 in range(2):
                        dst = bank[b][:, C * g2:C * g2 + C]
                        mm(dst, Tt[b][:, g2, :], U8[:, bass.ds(2 * g + g2, 1), :].rearrange("p g c -> p (g c)"),
                           start=True, stop=False)
                        for r in range(2):
                            ins = mm(dst, CAy[b][:, r, g2, :],
                                     Hs[:, r, bass.ds(g, 1), 0:C].rearrange("p g c -> p (g c)"),
                                     start=False, stop=r == 1)
                    ins.then_inc(y_done, 1)
            pe.wait_ge(y_out, GP + 4)
            with pe.Fori(0, NPAIR // 2) as i:
                for b in range(2):
                    m = 2 * i + b
                    kT = lambda n: qkv[:, bass.ds(8 * T + m * T, n)]
                    kTs = qkv[:, bass.ds(8 * T + m * T + TP, TS)]

                    def score(u):
                        hh, j = divmod(u, 5)
                        pe.wait_ge(sc_used, m * NU + u + 1)
                        if j < 4:
                            ins = mm(bank[u % 2][:, 0:P * (j + 1)], qz[b][:, hh, P * j:P * j + P], kT(P * (j + 1)),
                                     start=True, stop=True)
                        else:
                            mm(bank[u % 2][0:TS, :], qz[b][:, hh, TP:T], cK[b], start=True, stop=True)
                            ins = mm(bank[2][0:TS, 0:TS], qz[b][:, hh, TP:T], kTs, start=True, stop=True)
                        ins.then_inc(sc_done, 1)

                    pe.wait_ge(vs_ready, m + 1)
                    pe.wait_ge(vt_out, m + 1)
                    for k in range(4):
                        nc.tensor.transpose(acc[:, 1024 + P * k:1024 + P * k + P], vs[:, P * k:P * k + P], ident)
                    nc.tensor.transpose(acc[0:TS, 512:640], vs[:, TP:T], ident).then_inc(vt_done, 1)
                    pe.wait_ge(qz_ready, m + 1)
                    pe.wait_ge(a_in[b], 48 * i + 48)
                    score(0)
                    score(1)
                    for u in range(NU):
                        hh, j = divmod(u, 5)
                        S, tp = St[u % 2], acc[:, 512 * (u % 2):512 * (u % 2) + 512]
                        pe.wait_ge(p_ready, m * NU + u + 1)
                        pe.wait_ge(pt_out, m * NU + u + 1)
                        if j < 4:
                            for k in range(j + 1):
                                ins = nc.tensor.transpose(tp[:, P * k:P * k + P], S[:, P * k:P * k + P], ident)
                        else:
                            carrier()
                            for k in range(4):
                                nc.tensor.transpose(tp[:, TS * k:TS * k + TS], S[0:TS, P * k:P * k + P],
                                                    ident[0:TS, 0:TS])
                            ins = nc.tensor.transpose(tp[0:TS, 256:256 + TS], S[0:TS, TP:T], ident[0:TS, 0:TS])
                        ins.then_inc(pt_done, 1)
                        if u + 2 < NU:
                            score(u + 2)
                        if u == 0:
                            pe.wait_ge(vt_out, m + 2)
                            pe.wait_ge(o_out, m + 1)
                        pe.wait_ge(pt_out, m * NU + u + 3)
                        hs_ = slice(64 * hh, 64 * hh + 64)
                        if j < 4:
                            for k in range(j + 1):
                                ins = mm(acc[hs_, 1536 + P * j:1536 + P * j + P], Vs[b][:, k, hs_], PT[u % 2][:, k, :],
                                         start=k == 0, stop=k == j)
                        else:
                            for k in range(4):
                                mm(bank[3][hs_, 0:TS], cV[b][:, k, hs_], PT[u % 2][:, k, 0:TS], start=k == 0, stop=False)
                            ins = mm(bank[3][hs_, 0:TS], Vs[b][0:TS, 4, hs_], PT[u % 2][0:TS, 4, 0:TS],
                                     start=False, stop=True)
                        ins.then_inc(o_done, 1)
                    pe.wait_ge(o_done, m * NU + NU + 2)
                    pe.sem_inc(pair_done, 1)
            pe.wait_ge(gw_ready, 1)
            for m in range(8):
                pe.wait_ge(gelu_done, m + 1)
                if m >= 2:
                    pe.wait_ge(sig_done, m - 1)
                mm(bank[m % 2][:, :], GW[:, m, :], yT[:, m, 0:TP], start=True, stop=True)
                mm(bank[2 + m % 2][:, 0:TS], GW[:, m, :], yT[:, m, TP:T],
                   start=True, stop=True).then_inc(gate_done, 1)
            pe.wait_ge(sig_done, 8)
            for n in range(16):
                b = n // 8
                pe.wait_ge(sq_ready, n + 1)
                mm(bank[b][:, :], ones, sq[n % 2][:, 0:TP], start=n % 8 == 0, stop=n % 8 == 7)
                ins = mm(bank[2 + b][:, 0:TS], ones, sq[n % 2][:, TP:T], start=n % 8 == 0, stop=n % 8 == 7)
                ins.then_inc(sq_used, 1)
                if n % 8 == 7:
                    pe.wait_ge(sq_used, n + 1)
                    pe.sem_inc(ms_done, 1)
            pe.wait_ge(cat_ready, 2)
            cat = lambda k: (attT if k < 8 else yT)[:, k % 8, :]

            def mixed(first, group):
                c0, width = GROUPS[group]
                with pe.Fori(0, 8) as i:
                    for b in range(2):
                        pe.wait_ge(w_in[b], 16 * (first // 2 + 1 + i))
                        pe.wait_ge(slab_out, first + 2 * i + b + 1)
                        for k in range(KT):
                            ins = mm(bank[b][:, 0:width], wring[b][:, k, :], cat(k)[:, c0:c0 + width],
                                     start=k == 0, stop=k == KT - 1)
                        ins.then_inc(slab_done, 1)

            def ln1(t):
                t0, n = TILES[t]
                if t:
                    pe.wait_ge(res_ready, t)
                for f in range(KT):
                    ins = nc.tensor.transpose(acc[0:n, P * f:P * f + P], mixT[:, f, t0:t0 + n], ident)
                    if n < P:
                        ins = mm(acc[n:P, P * f:P * f + P], mixT[:, f, t0:t0 + n], ident, start=True, stop=True)
                ins.then_inc(mt_done, 1)
                pe.wait_ge(x1_ready, t + 1)
                for c in range(4):
                    if 4 * t + c >= 2:
                        pe.wait_ge(x1t_out, 4 * t + c - 1)
                    for q in range(4):
                        f = 4 * c + q
                        ins = nc.tensor.transpose(bank[c % 2][:, P * q:P * q + P], x1[:, t, P * f:P * f + P], ident)
                    ins.then_inc(x1t_done, 1)

            def scores(t):
                t0, n = TILES[t]
                if t:
                    pe.wait_ge(score_out, t)
                for c in range(4):
                    for q in range(4):
                        for r0 in range(0, P, n):
                            ins = mm(bank[c][r0:r0 + n, P * q:P * q + P], qpT[:, 4 * c + q, t0:t0 + n],
                                     keysT[:, 4 * c + q, :], start=True, stop=True)
                    ins.then_inc(score_done, 1)

            mixed(32, 0)
            pe.wait_ge(slab_out, 50)
            ln1(0)
            pe.wait_ge(x1t_out, 4)
            mixed(48, 0)
            pe.wait_ge(slab_out, 66)
            pe.wait_ge(keys_in, 32)
            scores(0)
            pe.wait_ge(score_out, 1)
            mixed(64, 1)
            pe.wait_ge(slab_out, 82)
            for t in range(1, NT):
                ln1(t)
            pe.wait_ge(x1t_out, 4 * NT)
            mixed(80, 1)
            pe.wait_ge(slab_out, 98)
            for seg in range(NT + 1):
                if seg + 1 < NT:
                    scores(seg + 1)
                if seg:
                    t = seg - 1
                    turns = STEPS[t] // RING
                    if t:
                        pe.wait_ge(ffn_read, t)

                    def step(i, j, first, final):
                        k = t * KK + RING * i + j
                        pe.wait_ge(diag_ready, k + 1)
                        pe.wait_ge(v_got[j], 16 * (t * (KK // RING) + i + 1))
                        for c in range(4):
                            ins = mm(acc[:, 512 * c:512 * c + 512], diag[j], vr[j][:, 512 * c:512 * c + 512],
                                     start=first, stop=final)
                        ins.then_inc(v_used, 1)

                    for j in range(RING):
                        step(0, j, j == 0, False)
                    with pe.Fori(1, turns - 1) as i:
                        for j in range(RING):
                            step(i, j, False, False)
                    for j in range(RING):
                        step(turns - 1, j, False, j == RING - 1)
                    pe.wait_ge(v_used, t * KK + STEPS[t] + RING)
                    pe.sem_inc(ffn_done, 1)


_INS = ["x_t", "x_tok", "w", "a_re", "a_im", "log_dt", "h0_re", "h0_im", "b_re", "b_im", "c_re", "c_im",
        "rel_bias", "ident", "block", "iota", "ssm_d", "glu_b", "g_attn", "g_ssm", "glu_w", "ck", "cv",
        "ln1_g", "ln1_b", "ln2_g", "ln2_b", "ident2", "keys_t", "peer_u", "peer_v"]
_OUTS = {"y": (T, D), "k_t": (1024, T), "v_t": (1024, T), "h": (P, 128)}


def _layouts(i):
    f = {k: np.asarray(v) for k, v in i.items()}
    tok = np.concatenate([f["x_prompt"][0], f["x_sample"][0]], axis=0)
    slab = lambda w: w.reshape(KT, P, -1, P).transpose(2, 1, 0, 3).reshape(-1, P, D)
    w_in = slab(f["w_in"][0])
    pair = lambda x: x.reshape(GP, 2 * SN).T
    pairh = lambda x: x.reshape(GP, 2 * SN, SG).transpose(1, 0, 2).reshape(P, GP * SG)
    feat = lambda x: x.reshape(8, P).T
    return {
        "x_t": tok.T, "x_tok": tok,
        "w": np.concatenate([w_in[24:], w_in[:24], slab(f["w_out"][0]), slab(f["peer_wq"][0])], axis=0),
        "a_re": pair(f["ssm_a_re"][0]), "a_im": pair(f["ssm_a_im"][0]),
        "log_dt": pair(np.broadcast_to(f["ssm_log_dt"][0][:, None], (GRP, SN))),
        "h0_re": pair(f["state_ssm_re"][0, 0]), "h0_im": pair(f["state_ssm_im"][0, 0]),
        "b_re": pairh(f["ssm_b_re"][0]), "b_im": pairh(f["ssm_b_im"][0]),
        "c_re": pairh(f["ssm_c_re"][0].transpose(0, 2, 1)), "c_im": pairh(f["ssm_c_im"][0].transpose(0, 2, 1)),
        "rel_bias": f["rel_bias"][0],
        "ident": np.eye(P, dtype=np.float32), "ident2": np.tile(np.eye(TS, dtype=np.float32), (2, 2)),
        "block": np.kron(np.eye(8, dtype=np.float32), np.ones((SG, SG), np.float32)),
        "iota": np.broadcast_to(np.arange(TOPK, dtype=np.float32), (P, TOPK)),
        "ssm_d": feat(f["ssm_d"][0]), "glu_b": feat(f["ssm_glu_b"][0]),
        "g_attn": feat(f["norm_attn_g"][0]), "g_ssm": feat(f["norm_ssm_g"][0]),
        "glu_w": f["ssm_glu_w"][0].reshape(8, P, SG).transpose(1, 0, 2).reshape(P, 8 * SG),
        "ck": f["cache_attn_k"][0, 0].reshape(TP, NPAIR, P).transpose(1, 2, 0),
        "cv": f["cache_attn_v"][0, 0].reshape(4, P, NPAIR, P).transpose(2, 1, 0, 3).reshape(NPAIR, P, TP),
        "ln1_g": f["ln1_g"][0], "ln1_b": f["ln1_b"][0], "ln2_g": f["ln2_g"][0], "ln2_b": f["ln2_b"][0],
        "keys_t": f["peer_keys"][0].transpose(3, 0, 1, 2).reshape(P, 16 * NKEY),
        "peer_u": f["peer_u"][0], "peer_v": f["peer_v"][0],
    }


def kernel(**inputs):
    import concourse.bacc as bacc
    from concourse.bass_utils import run_bass_kernel_spmd

    nc = bacc.Bacc("TRN2", target_bir_lowering=False, num_devices=1)
    laid = _layouts(inputs)
    arrays, a, o = {}, {}, {}
    for name in _INS:
        x = np.ascontiguousarray(laid[name])
        arrays[f"in_{name}"] = x
        a[name] = nc.dram_tensor(f"in_{name}", x.shape, mybir.dt.from_np(x.dtype), kind="ExternalInput").ap()
    for name, shape in _OUTS.items():
        o[name] = nc.dram_tensor(f"out_{name}", shape, F32, kind="ExternalOutput").ap()
    build(nc, a, o)
    got = run_bass_kernel_spmd(nc, [arrays], core_ids=[0]).results[0]
    y, kt, vt = (np.asarray(got[f"out_{n}"]) for n in ("y", "k_t", "v_t"))
    h = np.asarray(got["out_h"]).reshape(P, 2, 2, GP).transpose(1, 2, 3, 0).reshape(2, 2, GRP, SN)
    kv = lambda x, s: np.ascontiguousarray(x[:, s].T.reshape(1, 1, -1, H, DH))
    pr, sa = slice(0, TP), slice(TP, T)
    st_ = lambda s, r: np.ascontiguousarray(h[s, r].reshape(1, 1, GRP, SN))
    return (y[None, :TP], y[None, TP:], kv(kt, pr), kv(vt, pr), st_(0, 0), st_(0, 1),
            kv(kt, sa), kv(vt, sa), st_(1, 0), st_(1, 1))
```
